# Optimizing a Trainium2 kernel written in Bass

```python
import jax, jax.numpy as jnp
from jax import lax
import numpy as np

D_MODEL = 1024
BATCH = 1
SEQ = 512
DEPTH = 2

CHUNK = 64
N_A_LAYERS = DEPTH // 2
N_B_LAYERS = DEPTH - N_A_LAYERS
A_WIDTH = 2 * D_MODEL
A_GROUP_LEN = 128
A_HEAD_CH = 128
A_HEADS = A_WIDTH // A_HEAD_CH
B_HEAD_DIM = 64
B_HEADS = D_MODEL // B_HEAD_DIM
B_WIDTH = B_HEADS * B_HEAD_DIM
B_PREV_CHUNKS = 8
B_BAND = (B_PREV_CHUNKS + 1) * CHUNK
B_LEFT_PAD = B_PREV_CHUNKS * CHUNK
REL_CLIP = 256
N_REL = 2 * REL_CLIP + 1
EPS = 1e-6
NEG_INF = -1e30


def rms_norm(x, g):
    xf = x.astype(jnp.float32)
    y = xf * lax.rsqrt(jnp.mean(xf * xf, axis=-1, keepdims=True) + EPS)
    return (y * g.astype(jnp.float32)).astype(x.dtype)

def layer_norm(x, g, b):
    xf = x.astype(jnp.float32)
    mu = jnp.mean(xf, axis=-1, keepdims=True)
    xc = xf - mu
    y = xc * lax.rsqrt(jnp.mean(xc * xc, axis=-1, keepdims=True) + EPS)
    return (y * g.astype(jnp.float32) + b.astype(jnp.float32)).astype(x.dtype)

def gmlp_mixer(h, w_in, ln_g, ln_b, w_s, b_s, w_out):
    bsz, s, _ = h.shape
    u, v, z = jnp.split(h @ w_in, 3, axis=-1)
    u = jax.nn.gelu(u)
    v = layer_norm(jax.nn.gelu(v), ln_g, ln_b)
    vg = v.reshape(bsz, s // A_GROUP_LEN, A_GROUP_LEN, A_HEADS, A_HEAD_CH)
    pos_chunk = jnp.arange(A_GROUP_LEN) // CHUNK
    allowed = pos_chunk[:, None] >= pos_chunk[None, :]
    w_m = jnp.where(allowed[None], w_s, jnp.zeros_like(w_s)).astype(vg.dtype)
    mixed = jnp.einsum('hts,bgshc->bgthc', w_m, vg)
    mixed = mixed + b_s.T.astype(vg.dtype)[:, :, None]
    mixed = mixed.reshape(bsz, s, A_WIDTH)
    y = u * mixed * jax.nn.silu(z)
    return y @ w_out

def shared_kv(x, g_kv, w_kv):
    bsz, s, _ = x.shape
    k, v = jnp.split(rms_norm(x, g_kv) @ w_kv, 2, axis=-1)
    pad = ((0, 0), (B_LEFT_PAD, 0), (0, 0), (0, 0))
    k = jnp.pad(k.reshape(bsz, s, B_HEADS, B_HEAD_DIM), pad)
    v = jnp.pad(v.reshape(bsz, s, B_HEADS, B_HEAD_DIM), pad)
    return k, v

def chunk_attention_mixer(h, k_pad, v_pad, w_qz, rel_bias, w_out):
    bsz, s, _ = h.shape
    n_chunks = s // CHUNK
    q, z = jnp.split(h @ w_qz, 2, axis=-1)
    scale = B_HEAD_DIM ** -0.5
    q = (q * scale).reshape(bsz, n_chunks, CHUNK, B_HEADS, B_HEAD_DIM)
    q = jnp.moveaxis(q, 1, 0)
    qi = jnp.arange(CHUNK)
    m = jnp.arange(B_BAND)
    rel = qi[:, None] - m[None, :] + B_LEFT_PAD
    idx = jnp.clip(rel, -REL_CLIP, REL_CLIP) + REL_CLIP
    bias = rel_bias[:, idx].astype(jnp.float32)

    def one_chunk(args):
        c, qc = args
        start = c * CHUNK
        kc = lax.dynamic_slice_in_dim(k_pad, start, B_BAND, axis=1)
        vc = lax.dynamic_slice_in_dim(v_pad, start, B_BAND, axis=1)
        sc = jnp.einsum('bqhd,bkhd->bhqk', qc, kc).astype(jnp.float32) + bias
        valid = (m + start) >= B_LEFT_PAD
        sc = jnp.where(valid[None, None, None, :], sc, NEG_INF)
        p = jax.nn.softmax(sc, axis=-1).astype(vc.dtype)
        return jnp.einsum('bhqk,bkhd->bqhd', p, vc)

    o = lax.map(one_chunk, (jnp.arange(n_chunks), q))
    o = jnp.moveaxis(o, 0, 1).reshape(bsz, s, B_WIDTH)
    return (o * jax.nn.silu(z)) @ w_out

def first_inputs(seed: int = 0) -> dict:
    key = jax.random.key(seed)
    ks = jax.random.split(key, 20)
    f32 = jnp.float32
    nrm = lambda k, shp, sc: (jax.random.normal(k, shp, f32) * sc)
    x = jax.random.normal(ks[0], (BATCH, SEQ, D_MODEL), f32)
    a_norm_g = 1.0 + nrm(ks[1], (N_A_LAYERS, D_MODEL), 0.02)
    a_w_in = nrm(ks[2], (N_A_LAYERS, D_MODEL, 3 * A_WIDTH), D_MODEL ** -0.5)
    a_ln_g = 1.0 + nrm(ks[3], (N_A_LAYERS, A_WIDTH), 0.02)
    a_ln_b = nrm(ks[4], (N_A_LAYERS, A_WIDTH), 0.02)
    a_w_s = nrm(ks[5], (N_A_LAYERS, A_HEADS, A_GROUP_LEN, A_GROUP_LEN), A_GROUP_LEN ** -0.5)
    a_b_s = 1.0 + nrm(ks[6], (N_A_LAYERS, A_HEADS, A_GROUP_LEN), 0.1)
    a_w_out = nrm(ks[7], (N_A_LAYERS, A_WIDTH, D_MODEL), A_WIDTH ** -0.5)
    kv_norm_g = 1.0 + nrm(ks[8], (D_MODEL,), 0.02)
    w_kv = nrm(ks[9], (D_MODEL, 2 * B_WIDTH), D_MODEL ** -0.5)
    b_norm_g = 1.0 + nrm(ks[10], (N_B_LAYERS, D_MODEL), 0.02)
    b_w_qz = nrm(ks[11], (N_B_LAYERS, D_MODEL, 2 * B_WIDTH), D_MODEL ** -0.5)
    b_rel_bias = nrm(ks[12], (N_B_LAYERS, B_HEADS, N_REL), 0.5)
    b_w_out = nrm(ks[13], (N_B_LAYERS, B_WIDTH, D_MODEL), B_WIDTH ** -0.5)
    final_norm_g = 1.0 + nrm(ks[14], (D_MODEL,), 0.02)
    return {"x": x, "a_norm_g": a_norm_g, "a_w_in": a_w_in, "a_ln_g": a_ln_g,
            "a_ln_b": a_ln_b, "a_w_s": a_w_s, "a_b_s": a_b_s, "a_w_out": a_w_out,
            "kv_norm_g": kv_norm_g, "w_kv": w_kv, "b_norm_g": b_norm_g,
            "b_w_qz": b_w_qz, "b_rel_bias": b_rel_bias, "b_w_out": b_w_out,
            "final_norm_g": final_norm_g}

def first_block(x, a_norm_g, a_w_in, a_ln_g, a_ln_b, a_w_s, a_b_s, a_w_out,
              kv_norm_g, w_kv, b_norm_g, b_w_qz, b_rel_bias, b_w_out, final_norm_g):
    k_pad = None
    v_pad = None
    for layer in range(DEPTH):
        if layer < N_A_LAYERS:
            i = layer
            h = rms_norm(x, a_norm_g[i])
            x = x + gmlp_mixer(h, a_w_in[i], a_ln_g[i], a_ln_b[i], a_w_s[i],
                               a_b_s[i], a_w_out[i])
        else:
            i = layer - N_A_LAYERS
            if i == 0:
                k_pad, v_pad = shared_kv(x, kv_norm_g, w_kv)
            h = rms_norm(x, b_norm_g[i])
            x = x + chunk_attention_mixer(h, k_pad, v_pad, b_w_qz[i],
                                          b_rel_bias[i], b_w_out[i])
    return rms_norm(x, final_norm_g)


DEPTH_2 = 1

HG_HEADS = 8
HG_DIM = 128
HG_WIDTH = HG_HEADS * HG_DIM
HG_CHUNK = 32
MLA_HEADS = 8
QK_NOPE = 128
QK_ROPE = 64
QK_DIM = QK_NOPE + QK_ROPE
V_DIM = 128
Q_LORA = 3 * D_MODEL // 8
KV_LORA = D_MODEL // 4
MLA_WIDTH = MLA_HEADS * V_DIM
Q_BLOCK = 128
ROPE_THETA = 10000.0
N_BRANCH = 2
IN_SPLITS = (HG_WIDTH, HG_WIDTH, HG_WIDTH, HG_WIDTH,
             Q_LORA, KV_LORA, QK_ROPE, MLA_WIDTH,
             N_BRANCH * D_MODEL)
IN_COLS = sum(IN_SPLITS)


def _split_points():
    pts, acc = [], 0
    for w in IN_SPLITS[:-1]:
        acc += w
        pts.append(acc)
    return pts

def rms_norm_2(x, g):
    xf = x.astype(jnp.float32)
    y = xf * lax.rsqrt(jnp.mean(xf * xf, axis=-1, keepdims=True) + EPS)
    return (y * g.astype(jnp.float32)).astype(x.dtype)

def forget_lower_bounds(lb_logits):
    return jnp.cumsum(jax.nn.softmax(lb_logits.astype(jnp.float32), axis=0), axis=0)[:DEPTH_2]

def rope_tables(seq):
    inv = ROPE_THETA ** (-jnp.arange(0, QK_ROPE, 2, dtype=jnp.float32) / QK_ROPE)
    ang = jnp.arange(seq, dtype=jnp.float32)[:, None] * inv[None, :]
    return jnp.cos(ang), jnp.sin(ang)

def apply_rope(x, cos, sin):
    xf = x.astype(jnp.float32)
    x1, x2 = xf[..., : QK_ROPE // 2], xf[..., QK_ROPE // 2:]
    out = jnp.concatenate([x1 * cos - x2 * sin, x2 * cos + x1 * sin], axis=-1)
    return out.astype(x.dtype)

def hgrn2_recurrence(q, k, v, log_f):
    B, S, H, dk = q.shape
    dv = v.shape[-1]
    C = HG_CHUNK
    N = S // C

    def to_chunks(t):
        return t.reshape(B, N, C, H, t.shape[-1]).transpose(1, 0, 3, 2, 4)

    q, k, v, log_f = to_chunks(q), to_chunks(k), to_chunks(v), to_chunks(log_f)
    b = jnp.cumsum(log_f, axis=3)
    b_last = b[:, :, :, -1:, :]
    q_in = q * jnp.exp(b)
    k_in = k * jnp.exp(-b)
    k_out = k * jnp.exp(b_last - b)
    chunk_decay = jnp.exp(b_last[:, :, :, 0, :])

    causal = jnp.tril(jnp.ones((C, C), dtype=bool))
    scores = jnp.einsum('nbhtk,nbhsk->nbhts', q_in, k_in)
    scores = jnp.where(causal, scores, 0.0)
    o_intra = jnp.einsum('nbhts,nbhsv->nbhtv', scores, v)

    def step(state, inp):
        q_n, k_n, v_n, dec_n = inp
        o_inter = jnp.einsum('bhtk,bhkv->bhtv', q_n, state)
        state = state * dec_n[..., None] + jnp.einsum('bhsk,bhsv->bhkv', k_n, v_n)
        return state, o_inter

    state0 = jnp.zeros((B, H, dk, dv), jnp.float32)
    _, o_inter = lax.scan(step, state0, (q_in, k_out, v, chunk_decay))
    o = o_intra + o_inter
    return o.transpose(1, 0, 3, 2, 4).reshape(B, S, H, dv)

def hgrn2_branch(hq, hf, hi, hz, lb, hg_norm_g):
    B, S, _ = hq.shape
    dt = hq.dtype
    f = lb + (1.0 - lb) * jax.nn.sigmoid(hf.astype(jnp.float32))
    q = jax.nn.silu(hq.astype(jnp.float32)).reshape(B, S, HG_HEADS, HG_DIM)
    k = (1.0 - f).reshape(B, S, HG_HEADS, HG_DIM)
    v = hi.astype(jnp.float32).reshape(B, S, HG_HEADS, HG_DIM)
    log_f = jnp.log(f).reshape(B, S, HG_HEADS, HG_DIM)
    o = hgrn2_recurrence(q, k, v, log_f).astype(dt)
    o = rms_norm_2(o, hg_norm_g)
    o = o * jax.nn.silu(hz).reshape(B, S, HG_HEADS, HG_DIM)
    return o.reshape(B, S, HG_WIDTH)

def mla_branch(cq, ckv, kr, mz, q_a_g, w_uq, kv_a_g, w_ukv):
    B, S, _ = cq.shape
    cos, sin = rope_tables(S)
    q = (rms_norm_2(cq, q_a_g) @ w_uq).reshape(B, S, MLA_HEADS, QK_DIM)
    q_nope = q[..., :QK_NOPE]
    q_pe = apply_rope(q[..., QK_NOPE:], cos[:, None, :], sin[:, None, :])
    kv = (rms_norm_2(ckv, kv_a_g) @ w_ukv).reshape(B, S, MLA_HEADS, QK_NOPE + V_DIM)
    k_nope, v = kv[..., :QK_NOPE], kv[..., QK_NOPE:]
    k_pe = apply_rope(kr, cos, sin)
    scale = QK_DIM ** -0.5
    key_pos = jnp.arange(S)

    def attend_block(blk):
        start = blk * Q_BLOCK
        qn = lax.dynamic_slice_in_dim(q_nope, start, Q_BLOCK, axis=1)
        qp = lax.dynamic_slice_in_dim(q_pe, start, Q_BLOCK, axis=1)
        s = (jnp.einsum('bqhd,bkhd->bhqk', qn, k_nope)
             + jnp.einsum('bqhr,bkr->bhqk', qp, k_pe)).astype(jnp.float32) * scale
        q_pos = start + jnp.arange(Q_BLOCK)
        s = jnp.where(q_pos[:, None] >= key_pos[None, :], s, -jnp.inf)
        p = jax.nn.softmax(s, axis=-1).astype(v.dtype)
        return jnp.einsum('bhqk,bkhd->bqhd', p, v)

    out = lax.map(attend_block, jnp.arange(S // Q_BLOCK))
    out = out.transpose(1, 0, 2, 3, 4).reshape(B, S, MLA_WIDTH)
    return out * jax.nn.silu(mz)

def second_inputs(seed: int = 0) -> dict:
    key = jax.random.key(seed)
    ks = jax.random.split(key, 16)
    f32 = jnp.float32

    def w(k, shape, fan_in):
        return jax.random.normal(k, shape, f32) * fan_in ** -0.5

    def gain(k, shape):
        return 1.0 + 0.02 * jax.random.normal(k, shape, f32)

    return {
        "x": jax.random.normal(ks[0], (BATCH, SEQ, D_MODEL), f32),
        "norm_g": gain(ks[1], (DEPTH_2, D_MODEL)),
        "w_in": w(ks[2], (DEPTH_2, D_MODEL, IN_COLS), D_MODEL),
        "b_gate": 0.02 * jax.random.normal(ks[3], (DEPTH_2, N_BRANCH * D_MODEL), f32),
        "lb_logits": 0.1 * jax.random.normal(ks[4], (DEPTH_2 + 1, HG_WIDTH), f32),
        "hg_norm_g": gain(ks[5], (DEPTH_2, HG_DIM)),
        "q_a_g": gain(ks[6], (DEPTH_2, Q_LORA)),
        "w_uq": w(ks[7], (DEPTH_2, Q_LORA, MLA_HEADS * QK_DIM), Q_LORA),
        "kv_a_g": gain(ks[8], (DEPTH_2, KV_LORA)),
        "w_ukv": w(ks[9], (DEPTH_2, KV_LORA, MLA_HEADS * (QK_NOPE + V_DIM)), KV_LORA),
        "w_proj_a": w(ks[10], (DEPTH_2, HG_WIDTH, D_MODEL), HG_WIDTH),
        "w_proj_b": w(ks[11], (DEPTH_2, MLA_WIDTH, D_MODEL), MLA_WIDTH),
        "w_out": w(ks[12], (DEPTH_2, D_MODEL, D_MODEL), D_MODEL),
        "final_norm_g": gain(ks[13], (D_MODEL,)),
    }

def second_block(x, norm_g, w_in, b_gate, lb_logits, hg_norm_g, q_a_g, w_uq, kv_a_g, w_ukv,
              w_proj_a, w_proj_b, w_out, final_norm_g):
    B, S, _ = x.shape
    lower_bounds = forget_lower_bounds(lb_logits)
    pts = _split_points()
    for l in range(DEPTH_2):
        h = rms_norm_2(x, norm_g[l])
        proj = h @ w_in[l]
        hq, hf, hi, hz, cq, ckv, kr, mz, glog = jnp.split(proj, pts, axis=-1)
        y_a = hgrn2_branch(hq, hf, hi, hz, lower_bounds[l], hg_norm_g[l])
        y_b = mla_branch(cq, ckv, kr, mz, q_a_g[l], w_uq[l], kv_a_g[l], w_ukv[l])
        gates = jax.nn.sigmoid((glog + b_gate[l]).astype(jnp.float32)).astype(x.dtype)
        gates = gates.reshape(B, S, N_BRANCH, D_MODEL)
        merged = gates[:, :, 0] * (y_a @ w_proj_a[l]) + gates[:, :, 1] * (y_b @ w_proj_b[l])
        x = x + merged @ w_out[l]
    return rms_norm_2(x, final_norm_g)


def setup_inputs(seed=0):
    out = dict(first_inputs(seed))
    for name, value in second_inputs(seed + 1).items():
        if name != "x":
            out[name + "_2"] = value
    return out


def reference(
    x, a_norm_g, a_w_in, a_ln_g, a_ln_b, a_w_s, a_b_s, a_w_out, kv_norm_g, w_kv, b_norm_g,
    b_w_qz, b_rel_bias, b_w_out, final_norm_g, norm_g_2, w_in_2, b_gate_2, lb_logits_2,
    hg_norm_g_2, q_a_g_2, w_uq_2, kv_a_g_2, w_ukv_2, w_proj_a_2, w_proj_b_2, w_out_2,
    final_norm_g_2,
):
    x = first_block(
        x, a_norm_g, a_w_in, a_ln_g, a_ln_b, a_w_s, a_b_s, a_w_out, kv_norm_g, w_kv, b_norm_g,
        b_w_qz, b_rel_bias, b_w_out, final_norm_g,
    )
    return second_block(
        x, norm_g_2, w_in_2, b_gate_2, lb_logits_2, hg_norm_g_2, q_a_g_2, w_uq_2, kv_a_g_2,
        w_ukv_2, w_proj_a_2, w_proj_b_2, w_out_2, final_norm_g_2,
    )


_drawn_inputs = setup_inputs


def setup_inputs(seed=0):
    import zlib

    import numpy as np

    out = dict(_drawn_inputs(seed))
    spreads = {}
    factors = {'a_norm_g': 3.305,
     'a_ln_g': 8.0,
     'a_ln_b': 8.0,
     'kv_norm_g': 8.0,
     'b_norm_g': 8.0,
     'final_norm_g': 2.71,
     'norm_g_2': 5.962,
     'b_gate_2': 8.0,
     'lb_logits_2': 8.0,
     'hg_norm_g_2': 28.646,
     'q_a_g_2': 8.0,
     'kv_a_g_2': 8.0,
     'final_norm_g_2': 7.745}
    for name, (base, spread) in spreads.items():
        noise = np.random.default_rng([zlib.crc32(name.encode()), seed]).standard_normal(out[name].shape)
        drawn = base * np.exp(spread * noise) if base else spread * noise
        out[name] = __import__('jax').numpy.asarray(drawn.astype(out[name].dtype))
    for name, factor in factors.items():
        out[name] = (out[name] * factor).astype(out[name].dtype)
    return out
```

```python
from contextlib import ExitStack

import numpy as np

import concourse.bass as bass
from concourse import mybir

F32 = mybir.dt.float32
F32R = mybir.dt.float32r
U32 = mybir.dt.uint32
ALU = mybir.AluOpType
ACT = mybir.ActivationFunctionType

P = 128
S = 512
D = 1024
KT = D // P
TT = S // P
AW = 2048
AH = AW // P
BH, BD = 16, 64
PAIRS = BH // 2
RELX = 640
HH = 8
HC = 32
NCH = S // HC
MH = 8
QL, KL = 3, 2
NOPE, ROPE = 128, 64
EPS = 1e-6
NEG = -1e30

SLAB = 1024
LOOKAHEAD = 3
ROUNDS = {"v": 4, "uz": 8, "w1": 4, "at": 8, "w2": 2, "hg": 8, "dn": 2, "ml": 6, "mg": 8, "w3": 2}
FIRST, _at = {}, 0
for _name, _rounds in ROUNDS.items():
    FIRST[_name] = _at
    _at += _rounds
NR = _at
NSLAB = 4 * NR

VEC, _at = {}, 0
for _name, _cols in [("a_g", KT), ("ln_g", AH), ("ln_b", AH), ("kv_g", KT), ("b_g", KT), ("fin1", KT),
                     ("n2_g", KT), ("gate", 2 * KT), ("lb0", HH), ("lb1", HH), ("hg_g", 1), ("qa_g", QL),
                     ("kva_g", KL), ("fin2", KT)]:
    VEC[_name] = _at
    _at += _cols
NVEC = _at

QW = [P * (q + 1) for q in range(TT)]
QO = [sum(QW[:q]) for q in range(TT)]
SW = sum(QW)
KW = [S - P * k for k in range(TT)]
KO = [sum(KW[:k]) for k in range(TT)]


class Steps:

    def __init__(self, sem, names, rounds=1, prime=0):
        self.sem, self.names, self.rounds, self.prime = sem, list(names), rounds, prime
        self.n, self.next = len(self.names), 0
        assert len(set(self.names)) == self.n

    def did(self, name):
        assert self.names[self.next % self.n] == name, (name, self.names[self.next % self.n])
        self.next += 1
        return self.sem

    def at(self, name, r=0):
        return (r + self.prime) * self.n + (self.names.index(name) + 1)

    def all(self):
        return (self.rounds + self.prime) * self.n


def build(nc, xt, w, vecs, ws, bs, relx, consts, masks_hg, masks_ml, xs, rel_tab, out):
    ctx = ExitStack()
    with ctx:
        def sb(name, shape, dt, where=ctx):
            return where.enter_context(nc.sbuf_tensor(name, shape, dt))

        def sem(name):
            return ctx.enter_context(nc.semaphore(name))

        vec = sb("vec", [P, NVEC], F32)
        cst = sb("cst", [P, 2 * P], F32)
        ident, ones = cst[:, 0:P], cst[:, P:2 * P]
        lb = sb("lb", [P, 4, HH], F32)
        carry = sb("carry", [P, 4], F32)
        raw = sb("raw", [P, 2, SLAB], F32)
        whi = sb("whi", [P, 4, SLAB], F32R)
        wlo = sb("wlo", [P, 4, SLAB], F32R)
        hhi = sb("hhi", [P, KT, S], F32R)
        hlo = sb("hlo", [P, KT, S], F32R)
        yhi = sb("yhi", [P, AH, S], F32R)
        ylo = sb("ylo", [P, AH, S], F32R)

        with ExitStack() as scope:
            x = sb("x", [P, KT, S], F32, scope)
            nsq = sb("nsq", [P, 2, S], F32, scope)
            nacc = sb("nacc", [P, S], F32, scope)
            nr = sb("nr", [P, 2, S], F32, scope)
            nfull = sb("nfull", [P, 3, S], F32, scope)
            bb = sb("bb", [P, AH, P], F32, scope)
            wt_all = sb("wt_all", [P, AH, P], F32, scope)
        with ExitStack() as scope:
            vraw = sb("vraw", [P, TT, AW], F32, scope)
            sb("room_bb", [P, AH, P], F32, scope)
            stats = sb("stats", [P, TT, 4, 6], F32, scope)
            mv = sb("mv", [P, TT, 2], F32, scope)
            rstd = sb("rstd", [P, 4, TT], F32, scope)
            vhi = sb("vhi", [P, TT, 2 * P], F32R, scope)
            vlo = sb("vlo", [P, TT, 2 * P], F32R, scope)
            wt = sb("wt", [P, 2, P], F32, scope)
            wthi = sb("wthi", [P, 2, P], F32R, scope)
            wtlo = sb("wtlo", [P, 2, P], F32R, scope)
            mt = sb("mt", [P, 2, S], F32, scope)
            ug = sb("ug", [P, 2, S], F32, scope)
            sz = sb("sz", [P, 2, S], F32, scope)
        with ExitStack() as scope:
            sb("room_x1", [P, KT, S], F32, scope)
            khi = sb("khi", [P, S], F32R, scope)
            klo = sb("klo", [P, S], F32R, scope)
            qhi = sb("qhi", [P, S], F32R, scope)
            qlo = sb("qlo", [P, S], F32R, scope)
            avhi = sb("avhi", [P, TT, P], F32R, scope)
            avlo = sb("avlo", [P, TT, P], F32R, scope)
            avf = sb("avf", [P, S], F32, scope)
            az = sb("az", [P, S], F32, scope)
            ay = sb("ay", [P, S], F32, scope)
            sc = sb("sc", [P, 2, SW], F32, scope)
            phi = sb("phi", [P, 2, SW], F32R, scope)
            plo = sb("plo", [P, 2, SW], F32R, scope)
            tab = sb("tab", [P, 2, S], F32, scope)
            sm = sb("sm", [P, 2, 4, TT], F32, scope)
        with ExitStack() as scope:
            he = sb("he", [P, S], F32, scope)
            hf = sb("hf", [P, S], F32, scope)
            hk = sb("hk", [P, S], F32, scope)
            hb = sb("hb", [P, S], F32, scope)
            hd = sb("hd", [P, S], F32, scope)
            heb = sb("heb", [P, S], F32, scope)
            hen = sb("hen", [P, S], F32, scope)
            hq = sb("hq", [P, S], F32, scope)
            hv = sb("hv", [P, S], F32, scope)
            hdec = sb("hdec", [P, NCH], F32, scope)
            hkhi = sb("hkhi", [P, S], F32R, scope)
            hklo = sb("hklo", [P, S], F32R, scope)
            hs = sb("hs", [P, S], F32, scope)
            hshi = sb("hshi", [P, S], F32R, scope)
            hslo = sb("hslo", [P, S], F32R, scope)
            hst = sb("hst", [P, 2, 4, P], F32, scope)
            hz = sb("hz", [P, 2, S], F32, scope)
            ho = sb("ho", [P, 2, S], F32, scope)
            hm = sb("hm", [P, 2, S], F32, scope)
        hqin = [yhi[:, 8:10, :], ylo[:, 8:10, :]]
        hvv = [yhi[:, 10, :], ylo[:, 10, :]]
        hko = [yhi[:, 11, :], ylo[:, 11, :]]
        hss = [t[:, 12:16, :].rearrange("p a (b v) -> p (a b) v", v=P) for t in (yhi, ylo)]
        with ExitStack() as scope:
            lhi = sb("lhi", [P, QL + KL, S], F32R, scope)
            llo = sb("llo", [P, QL + KL, S], F32R, scope)
            mkp = sb("mkp", [ROPE, 2, S], F32R, scope)
            mm = sb("mm", [P, 2, S], F32, scope)
            mt1 = sb("mt1", [ROPE, 2, S], F32, scope)
            with ExitStack() as part:
                dsq = sb("dsq", [P, QL + KL, S], F32, part)
                dr = sb("dr", [P, 2, 2, S], F32, part)
            with ExitStack() as part:
                mq = sb("mq", [P, 2, S], F32R, part)
                mqp = sb("mqp", [ROPE, 2, S], F32R, part)
                mk = sb("mk", [P, 2, S], F32R, part)
                mv2 = sb("mv2", [P, 2, S], F32R, part)
                mz = sb("mz", [P, S], F32, part)
                my = sb("my", [P, S], F32, part)
                msc = sb("msc", [P, SW], F32, part)
                mph = sb("mph", [P, SW], F32R, part)
                mpl = sb("mpl", [P, SW], F32R, part)
                msm = sb("msm", [P, 4, TT], F32, part)
        with ExitStack() as scope:
            sb("room_x2", [P, KT, S], F32, scope)
            mga = sb("mga", [P, 2, S], F32, scope)
            sb("room_n", [P, 6, S], F32, scope)
            mgh = sb("mgh", [P, KT, S], F32R, scope)
            mgl = sb("mgl", [P, KT, S], F32R, scope)

        bank = [ctx.enter_context(nc.psum_tensor(f"bank{i}", [P, S], F32)) for i in range(8)]

        raw_loaded = [sem("raw_loaded0"), sem("raw_loaded1")]
        hi_done = sem("hi_done")
        lo_done = sem("lo_done")
        slab_used = sem("slab_used")

        ld_vec, ld_x, ld_ws, ld_bs, ld_wt = sem("ld_vec"), sem("ld_x"), sem("ld_ws"), sem("ld_bs"), sem("ld_wt")
        ld_x1, ld_tab, ld_hm, ld_mm, ld_x3 = sem("ld_x1"), [sem("ld_tab0"), sem("ld_tab1")], sem("ld_hm"), sem("ld_mm"), sem("ld_x3")
        st_x, st_rel, st_out = sem("st_x"), sem("st_rel"), sem("st_out")

        all_steps = []

        def steps(name, names, rounds=1, prime=0):
            s = Steps(sem(name), names, rounds, prime)
            all_steps.append(s)
            return s

        def numbered(name, n):
            return [f"{name}{i}" for i in range(n)]

        proP = steps("pro_pe", ["rowsum"])
        proA = steps("pro_act", ["exp"] + numbered("sq", KT))
        proV = steps("pro_dve", ["mask", "zero", "max", "sub0", "sub1", "sum", "inv", "low", "high"]
                     + numbered("acc", KT) + ["bb"])

        def norm_steps(name, n, cut, squares=False):
            v = ["mean", "inv"]
            for t in range(n + 1):
                v += [f"full{t}"] if t < n else []
                if t >= 1:
                    v += [f"lo{t - 1}"] if cut else [f"acc{t - 1}"] if squares else []
            a = ["root"] + (numbered("hi", n) if cut else numbered("sq", n) if squares else [])
            return steps(name + "_pe", ["ms"]), steps(name + "_act", a), steps(name + "_dve", v)

        n0 = norm_steps("n0", KT, True)
        nb = norm_steps("nb", 2 * KT, True)
        nf = norm_steps("nf", KT, False, True)
        n2 = norm_steps("n2", KT, True)
        n3 = norm_steps("n3", KT, False)

        vA = steps("v_act", numbered("gelu", TT), ROUNDS["v"], prime=2)
        vV = steps("v_dve", numbered("stats", TT), ROUNDS["v"])
        vaA = steps("va_act", ["root"])
        vaV = steps("va_dve", ["mask", "aggr", "eps", "inv", "shift"])
        uzP = steps("uz_pe", ["mix0", "mix1", "turn0", "turn1"], ROUNDS["uz"], prime=1)
        uzA = steps("uz_act", ["vhi", "whi", "u0", "u1", "mixed0", "mixed1", "z0", "z1"], ROUNDS["uz"], prime=1)
        uzV = steps("uz_dve", ["norm", "vlo", "wlo"] + [f"{n}{q}" for q in range(2)
                    for n in ("affine", "gate", "y", "yhi", "ylo")], ROUNDS["uz"], prime=1)
        w1A = steps("w1_act", ["sq0", "sq1"], ROUNDS["w1"])
        w1V = steps("w1_dve", ["x0", "acc0", "x1", "acc1"], ROUNDS["w1"], prime=1)
        w1Z = steps("w1_zero", ["zero"])
        atP = steps("at_pe", ["s0", "s1", "t0", "vt", "t1", "o0", "o1"], ROUNDS["at"])
        atA = steps("at_act", ["khi", "qhi", "exp0", "v", "phi0", "vhi", "exp1", "ez", "phi1"], ROUNDS["at"])
        atV = steps("at_dve", ["klo", "qlo", "max0", "neg0", "inv0", "p0", "max1", "neg1", "plo0", "vlo", "inv1",
                               "p1", "z1p", "zinv", "z", "plo1", "y0", "y1", "yhi", "ylo"], ROUNDS["at"], prime=1)
        atM = steps("at_mask", ["mask"])
        w2A = steps("w2_act", numbered("sq", KT))
        w2V = steps("w2_dve", ["zero"] + [f"{n}{m}" for m in range(KT) for n in ("x", "acc")])
        hpA = steps("hp_act", ["ef", "log", "eb", "en", "ed", "eq", "khi", "qhi", "v", "ez"], HH, prime=1)
        hpV = steps("hp_dve", ["f1p", "finv", "f", "k", "b", "rest", "q1p", "qinv", "q", "qin", "kin", "kout", "klo",
                               "qlo", "dec", "z1p", "zinv", "z"], HH, prime=1)
        htP = steps("ht_pe", ["vt", "kt", "s", "u", "o", "ms"], HH)
        htA = steps("ht_act", ["vhi", "kohi", "shi"] + numbered("sthi", 4) + ["sq"], HH)
        htV = steps("ht_dve", ["vlo", "kolo", "s", "slo"]
                    + [n for b in range(4) for n in [f"st{i}" for i in range(4 * b + 1, min(4 * b + 5, NCH))] + [f"stlo{b}"]],
                    HH)
        hoA = steps("ho_act", ["root"], HH)
        hoV = steps("ho_dve", ["mean", "inv", "norm", "y", "yhi", "ylo"], HH, prime=1)
        hzV = steps("hz_dve", ["zero"])
        dnP = steps("dn_pe", ["msq", "msk"])
        dnA = steps("dn_act", numbered("sq", QL + KL) + ["rq", "rk"] + numbered("hi", QL + KL) + ["kphi"])
        dnV = steps("dn_dve", ["turn", "straight", "kp", "mq", "iq", "mk", "ik"] + numbered("full", QL + KL)
                    + numbered("lo", QL + KL) + ["kplo"])
        mlP = steps("ml_pe", ["s", "t", "o"], MH)
        mlA = steps("ml_act", ["qhi", "khi", "vhi", "qphi", "exp", "ez", "phi"], MH)
        mlV = steps("ml_dve", ["turn", "straight", "qp", "qlo", "klo", "vlo", "qplo", "max", "neg", "inv", "p", "z1p",
                               "zinv", "z", "plo", "y", "yhi", "ylo"], MH, prime=1)
        mgA = steps("mg_act", ["g0", "g1"], ROUNDS["mg"], prime=1)
        mgV = steps("mg_dve", ["a", "b", "sum", "hi", "lo"], ROUNDS["mg"], prime=1)
        w3A = steps("w3_act", numbered("sq", KT))
        w3V = steps("w3_dve", ["zero"] + [f"{n}{m}" for m in range(KT) for n in ("x", "acc")])

        def prime(eng, those):
            for s in those:
                if s.prime:
                    eng.sem_inc(s.sem, s.prime * s.n)

        def col(name, i=0):
            return vec[:, bass.ds(VEC[name] + i, 1)]

        def f32(ap):
            return ap.bitcast(F32)

        block = ctx.enter_context(nc.Block())

        @block.sync
        def _(sp):
            for n in range(4):
                if n >= 2:
                    sp.wait_ge(lo_done, n - 1)
                sp.dma_start(raw[:, n % 2, :], w[n, :, :]).then_inc(raw_loaded[n % 2], 16)
            with sp.Fori(1, NR) as r:
                for j in range(4):
                    sp.wait_ge(lo_done, 4 * r + j - 1)
                    sp.dma_start(raw[:, j % 2, :], w[4 * r + j, :, :]).then_inc(raw_loaded[j % 2], 16)
            for t in range(KT):
                sp.wait_ge(n3[2].sem, n3[2].at(f"full{t}"))
                sp.dma_start(out[t, :, :], x[:, t, :]).then_inc(st_out, 16)
            sp.wait_ge(st_out, 16 * KT)

        @block.gpsimd
        def _(pool):
            with pool.Fori(0, NR) as r:
                for j in range(4):
                    pool.wait_ge(hi_done, 4 * r + j + 1)
                    nc.gpsimd.tensor_tensor(wlo[:, j, :], raw[:, j % 2, :], f32(whi[:, j, :]),
                                            ALU.subtract).then_inc(lo_done, 1)

        @block.tensor
        def _(pe):
            pe.sem_inc(slab_used, 1)
            prime(pe, [uzP])

            def mm3(dst, a, b, first, last):
                nc.tensor.matmul(dst, a[0], b[0], start=first, stop=False)
                nc.tensor.matmul(dst, a[1], b[0], start=False, stop=False)
                return nc.tensor.matmul(dst, a[0], b[1], start=False, stop=last)

            def slab(r, j, dst, rhs, first=True, last=True, count=1):
                pe.wait_ge(lo_done, 4 * r + j + 1)
                for k in range(KT):
                    a = [t[:, j, k * P:(k + 1) * P] for t in (whi, wlo)]
                    b = [t[:, k, :] for t in rhs]
                    done = mm3(dst[:, :], a, b, first and k == 0, last and k == KT - 1)
                done.then_inc(slab_used, count)

            def norm(steps_, ready, value):
                pe.wait_ge(ready, value)
                nc.tensor.matmul(bank[7][:, :], ones, nacc[:, :], start=True,
                                 stop=True).then_inc(steps_[0].did("ms"), 1)

            h = (hhi, hlo)
            y_lower = (yhi[:, 0:KT, :], ylo[:, 0:KT, :])
            y_upper = (yhi[:, KT:AH, :], ylo[:, KT:AH, :])

            pe.wait_ge(ld_vec, 32)
            pe.wait_ge(proV.sem, proV.at("mask"))
            for i in range(4):
                rs = nc.tensor.matmul(bank[i][:, :], ones, wt_all[:, 4 * i:4 * i + 4, :], start=True, stop=True)
            rs.then_inc(proP.did("rowsum"), 1)
            norm(n0, proV.sem, proV.at(f"acc{KT - 1}"))
            pe.wait_ge(proV.sem, proV.all())

            with pe.Fori(0, ROUNDS["v"] // 2) as i:
                for par in range(2):
                    r = 2 * i + par
                    for j in range(4):
                        pe.wait_ge(lo_done, 4 * r + j + 1)
                        for k in (2 * j, 2 * j + 1):
                            pe.wait_ge(n0[2].sem, n0[2].at(f"lo{k}"))
                            for t in range(TT):
                                if k == 0:
                                    pe.wait_ge(vA.sem, vA.at(f"gelu{t}", r - 2))
                                a = [u[:, k, t * P:(t + 1) * P] for u in h]
                                b = [u[:, j, (k % 2) * S:(k % 2 + 1) * S] for u in (whi, wlo)]
                                done = mm3(bank[4 * par + t][:, :], a, b, k == 0, k == KT - 1)
                        done.then_inc(slab_used, 1)

            pe.wait_ge(vA.sem, vA.all())
            with pe.Fori(0, ROUNDS["uz"]) as i:
                r = i + FIRST["uz"]
                pe.wait_ge(uzA.sem, uzA.at("u0", i - 1))
                slab(r, 0, bank[0], h)
                pe.wait_ge(uzA.sem, uzA.at("u1", i - 1))
                slab(r, 1, bank[1], h)
                pe.wait_ge(uzV.sem, uzV.at("wlo", i))
                for q in range(2):
                    pe.wait_ge(uzA.sem, uzA.at(f"mixed{q}", i - 1))
                    cols = slice(q * P, (q + 1) * P)
                    mm3(bank[4 + q][:, :], (wthi[:, q, :], wtlo[:, q, :]), (vhi[:, :, cols], vlo[:, :, cols]),
                        True, True).then_inc(uzP.did(f"mix{q}"), 1)
                for q in range(2):
                    pe.wait_ge(uzA.sem, uzA.at(f"z{q}", i - 1))
                    slab(r, 2 + q, bank[2 + q], h)
                    pe.wait_ge(uzA.sem, uzA.at(f"mixed{q}", i))
                    pe.wait_ge(uzV.sem, uzV.at(f"affine{q}", i - 1))
                    for t in range(TT):
                        turn = nc.tensor.transpose(bank[6 + q][:, t * P:(t + 1) * P], mt[:, q, t * P:(t + 1) * P],
                                                   ident)
                    turn.then_inc(uzP.did(f"turn{q}"), 1)

            pe.wait_ge(uzV.sem, uzV.all())
            pe.wait_ge(uzA.sem, uzA.all())
            with pe.Fori(0, ROUNDS["w1"]) as i:
                r = i + FIRST["w1"]
                for q in range(2):
                    pe.wait_ge(w1V.sem, w1V.at(f"x{q}", i - 1))
                    slab(r, 2 * q, bank[2 * q], y_lower, last=False)
                    slab(r, 2 * q + 1, bank[2 * q], y_upper, first=False)
            norm(nb, w1V.sem, w1V.all())

            with pe.Fori(0, ROUNDS["at"]) as i:
                r = i + FIRST["at"]

                def scores(q):
                    rows = slice(BD * q, BD * (q + 1))
                    for t, (b, c) in enumerate([(5, QW[2]), (6, 0), (5, 0), (4, 0)]):
                        last = mm3(bank[b][:, c:c + QW[t]], [u[rows, t * P:(t + 1) * P] for u in (qhi, qlo)],
                                   [u[rows, 0:QW[t]] for u in (khi, klo)], True, True)
                    last.then_inc(atP.did(f"s{q}"), 1)

                def turned(q):
                    for k in range(TT):
                        for t in range(k, TT):
                            b, c = [(7, 0), (0, 0), (1, 0), (1, KW[2])][k]
                            c += (t - k) * P
                            last = nc.tensor.transpose(bank[b][:, c:c + P],
                                                       sc[:, q, QO[t] + k * P:QO[t] + (k + 1) * P], ident)
                    last.then_inc(atP.did(f"t{q}"), 1)

                def attended(q):
                    for k in range(TT):
                        last = mm3(bank[4 + q][:, k * P:S], (avhi[:, k, :], avlo[:, k, :]),
                                   [u[:, q, KO[k]:KO[k] + KW[k]] for u in (phi, plo)], k == 0, k == TT - 1)
                    last.then_inc(atP.did(f"o{q}"), 1)

                pe.wait_ge(nb[2].sem, nb[2].at(f"lo{KT - 1}"))
                pe.wait_ge(atV.sem, atV.at("plo1", i - 1))
                slab(r, 0, bank[0], h)
                pe.wait_ge(nb[2].sem, nb[2].all())
                slab(r, 1, bank[1], y_upper)
                pe.wait_ge(atV.sem, atV.at("qlo", i))
                pe.wait_ge(atV.sem, atV.at("y1", i - 1))
                scores(0)
                slab(r, 2, bank[2], h)
                pe.wait_ge(atV.sem, atV.at("max0", i))
                scores(1)
                pe.wait_ge(atV.sem, atV.at("p0", i))
                turned(0)
                pe.wait_ge(atA.sem, atA.at("v", i))
                for t in range(TT):
                    last = nc.tensor.transpose(bank[2][:, t * P:(t + 1) * P], avf[:, t * P:(t + 1) * P], ident)
                last.then_inc(atP.did("vt"), 1)
                slab(r, 3, bank[3], y_upper)
                pe.wait_ge(atV.sem, atV.at("p1", i))
                turned(1)
                attended(0)
                pe.wait_ge(atV.sem, atV.at("plo1", i))
                attended(1)

            pe.wait_ge(atV.sem, atV.all())
            for m in range(KT):
                if m >= 4:
                    pe.wait_ge(w2V.sem, w2V.at(f"x{m - 4}"))
                slab(FIRST["w2"] + m // 4, m % 4, bank[m % 4], y_lower)
            norm(nf, w2V.sem, w2V.all())
            norm(n2, nf[2].sem, nf[2].all())

            def hg_project(r, jj):
                read, name = [(hpV, "f1p"), (hpV, "q"), (hpA, "v"), (hpV, "z")][jj]
                pe.wait_ge(read.sem, read.at(name, r - 1))
                slab(r + FIRST["hg"], jj, bank[jj], h)

            def hg_turn(s, par):
                pe.wait_ge(hpV.sem, hpV.at("z", s))
                pe.wait_ge(hpA.sem, hpA.at("ez", s))
                pe.wait_ge(hoV.sem, hoV.at("norm", s - 1))
                for t in range(TT):
                    last = nc.tensor.transpose(bank[4][:, t * P:(t + 1) * P], hv[:, t * P:(t + 1) * P], ident)
                last.then_inc(htP.did("vt"), 1)
                for t in range(TT):
                    last = nc.tensor.transpose(bank[5][:, t * P:(t + 1) * P], hd[:, t * P:(t + 1) * P], ident)
                last.then_inc(htP.did("kt"), 1)
                for t in range(TT):
                    cols = slice(t * P, (t + 1) * P)
                    last = mm3(bank[6][:, cols], (hkhi[:, cols], hklo[:, cols]),
                               [u[:, par, cols] for u in hqin], True, True)
                last.then_inc(htP.did("s"), 1)

            def hg_updates(s):
                pe.wait_ge(htV.sem, htV.at("s", s))
                for b in range(4):
                    for q in range(4 if b < 3 else 3):
                        rows, cols = slice(HC * q, HC * (q + 1)), slice(b * P, (b + 1) * P)
                        last = mm3(bank[4 + q][:, b * P:(b + 1) * P], [u[rows, cols] for u in hko],
                                   [u[rows, cols] for u in hvv], True, True)
                last.then_inc(htP.did("u"), 1)

            def hg_outputs(s, par):
                pe.wait_ge(htV.sem, htV.at("stlo3", s))
                for b in range(4):
                    cols = slice(b * P, (b + 1) * P)
                    mm3(bank[4][:, cols], [u[:, cols] for u in hvv], (hshi[:, cols], hslo[:, cols]), True, False)
                    for n in range(max(1, 4 * b), 4 * b + 4):
                        c = slice(n * HC, (n + 1) * HC)
                        last = mm3(bank[4][:, c], [u[:, n, :] for u in hss], [u[:, par, c] for u in hqin], False,
                                   n == 4 * b + 3)
                last.then_inc(htP.did("o"), 1)
                pe.wait_ge(htA.sem, htA.at("sq", s))
                nc.tensor.matmul(bank[5][:, :], ones, ho[:, 0, :], start=True, stop=True).then_inc(htP.did("ms"), 1)

            def hg_round(r, par, project, stage):
                if project:
                    hg_project(r, 0)
                if stage:
                    hg_turn(r - 1, 1 - par)
                if project:
                    hg_project(r, 1)
                if stage:
                    hg_updates(r - 1)
                if project:
                    hg_project(r, 2)
                    hg_project(r, 3)
                if stage:
                    hg_outputs(r - 1, 1 - par)

            pe.wait_ge(n2[2].sem, n2[2].all())
            hg_round(0, 0, True, False)
            with pe.Fori(0, (HH - 2) // 2) as i:
                hg_round(2 * i + 1, 1, True, True)
                hg_round(2 * i + 2, 0, True, True)
            hg_round(HH - 1, 1, True, True)
            hg_round(HH, 0, False, True)

            pe.wait_ge(hoV.sem, hoV.all())
            for n in range(6):
                if n == 5:
                    pe.wait_ge(lo_done, 4 * FIRST["dn"] + 8)
                slab(FIRST["dn"] + n // 4, n % 4, bank[n], h, count=3 if n == 5 else 1)
            for g, (b, t0, n) in enumerate([(6, 0, QL), (7, QL, KL)]):
                for t in range(t0, t0 + n):
                    pe.wait_ge(dnA.sem, dnA.at(f"sq{t}"))
                    last = nc.tensor.matmul(bank[b][:, :], ones, dsq[:, t, :], start=t == t0, stop=t == t0 + n - 1)
                last.then_inc(dnP.did(("msq", "msk")[g]), 1)

            pe.wait_ge(dnV.sem, dnV.all())
            with pe.Fori(0, MH // 4) as i:
                for g in range(4):
                    hd_ = 4 * i + g
                    r3 = 3 * i + FIRST["ml"]
                    n = 3 * g
                    pe.wait_ge(lo_done, 4 * (r3 + n // 4) + n % 4 + 1)
                    pe.wait_ge(mlV.sem, mlV.at("plo", hd_ - 1))
                    for b in range(2):
                        for k in range(QL):
                            c = (2 * k + b) * P
                            last = mm3(bank[b][:, :], [u[:, n % 4, c:c + P] for u in (whi, wlo)],
                                       (lhi[:, k, :], llo[:, k, :]), k == 0, k == QL - 1)
                    last.then_inc(slab_used, 1)
                    n = 3 * g + 1
                    pe.wait_ge(lo_done, 4 * (r3 + n // 4) + n % 4 + 1)
                    pe.wait_ge(mlV.sem, mlV.at("y", hd_ - 1))
                    for k in range(KL):
                        mm3(bank[2][:, :], [u[:, n % 4, 2 * k * P:(2 * k + 1) * P] for u in (whi, wlo)],
                            (lhi[:, QL + k, :], llo[:, QL + k, :]), k == 0, k == KL - 1)
                    for t in range(TT):
                        cols = slice(t * P, (t + 1) * P)
                        for k in range(KL):
                            last = mm3(bank[3][:, cols], (lhi[:, QL + k, cols], llo[:, QL + k, cols]),
                                       [u[:, n % 4, (2 * k + 1) * P:(2 * k + 2) * P] for u in (whi, wlo)],
                                       k == 0, k == KL - 1)
                    last.then_inc(slab_used, 1)
                    pe.wait_ge(mlV.sem, mlV.at("qplo", hd_))
                    for t, (b, c) in enumerate([(5, QW[2]), (6, 0), (5, 0), (4, 0)]):
                        cols = slice(t * P, (t + 1) * P)
                        mm3(bank[b][:, c:c + QW[t]], (mq[:, 0, cols], mq[:, 1, cols]),
                            (mk[:, 0, 0:QW[t]], mk[:, 1, 0:QW[t]]), True, False)
                        last = mm3(bank[b][:, c:c + QW[t]], (mqp[:, 0, cols], mqp[:, 1, cols]),
                                   (mkp[:, 0, 0:QW[t]], mkp[:, 1, 0:QW[t]]), False, True)
                    last.then_inc(mlP.did("s"), 1)
                    n = 3 * g + 2
                    slab(r3 + n // 4, n % 4, bank[2], h)
                    pe.wait_ge(mlV.sem, mlV.at("p", hd_))
                    for k in range(TT):
                        for t in range(k, TT):
                            b, c = [(7, 0), (0, 0), (1, 0), (1, KW[2])][k]
                            c += (t - k) * P
                            last = nc.tensor.transpose(bank[b][:, c:c + P],
                                                       msc[:, QO[t] + k * P:QO[t] + (k + 1) * P], ident)
                    last.then_inc(mlP.did("t"), 1)
                    pe.wait_ge(mlV.sem, mlV.at("plo", hd_))
                    for k in range(TT):
                        cols = slice(k * P, (k + 1) * P)
                        last = mm3(bank[3][:, k * P:S], (mv2[:, 0, cols], mv2[:, 1, cols]),
                                   [u[:, KO[k]:KO[k] + KW[k]] for u in (mph, mpl)], k == 0, k == TT - 1)
                    last.then_inc(mlP.did("o"), 1)

            pe.wait_ge(mlV.sem, mlV.all())
            with pe.Fori(0, ROUNDS["mg"]) as i:
                r = i + FIRST["mg"]
                for j, (rhs, st, name) in enumerate([(h, mgA, "g0"), (h, mgA, "g1"), (y_lower, mgV, "a"),
                                                     (y_upper, mgV, "b")]):
                    pe.wait_ge(st.sem, st.at(name, i - 1))
                    slab(r, j, bank[j], rhs)

            pe.wait_ge(mgV.sem, mgV.all())
            for m in range(KT):
                if m >= 4:
                    pe.wait_ge(w3V.sem, w3V.at(f"x{m - 4}"))
                slab(FIRST["w3"] + m // 4, m % 4, bank[m % 4], (mgh, mgl))
            norm(n3, w3V.sem, w3V.all())

        @block.scalar
        def _(act):
            act.dma_start(vec[:, :], vecs).then_inc(ld_vec, 16)
            act.dma_start(cst[:, :], consts).then_inc(ld_vec, 16)
            act.dma_start(x[:, :, :], xt).then_inc(ld_x, 16)
            act.dma_start(wt_all[:, :, :], ws[:, 0:AH, :]).then_inc(ld_ws, 16)
            act.dma_start(bb[:, :, :], bs.partition_broadcast(P)).then_inc(ld_bs, 16)
            act.dma_start(rel_tab[0:BH, :, :], bass.AP(relx.tensor, P - 1,
                                                      [[RELX, BH], [-1, P], [1, S]])).then_inc(st_rel, 16)
            act.dma_start(rel_tab[BH:BH + 2, :, :], bass.AP(relx.tensor, P - 1,
                                                            [[RELX, 2], [-1, P], [1, S]])).then_inc(st_rel, 16)
            prime(act, [vA, uzA, mgA, hpA])

            def cut(r, j):
                if isinstance(r, int) and 4 * r + j + LOOKAHEAD >= NSLAB:
                    return
                slot = (j + LOOKAHEAD) % 4
                act.wait_ge(raw_loaded[slot % 2], 16 * (2 * r + (j + LOOKAHEAD) // 2 + 1))
                act.wait_ge(slab_used, 4 * r + j + 1)
                nc.scalar.activation(whi[:, slot, :], raw[:, slot % 2, :], ACT.Copy).then_inc(hi_done, 1)

            def used(r, j):
                act.wait_ge(slab_used, 4 * r + j + 2)

            def norm(steps_, outs, squares=False):
                _, a, v = steps_
                act.wait_ge(v.sem, v.at("inv"))
                nc.scalar.activation(nr[:, 0, :], nr[:, 1, :], ACT.Sqrt).then_inc(a.did("root"), 1)
                for t, o in enumerate(outs):
                    act.wait_ge(v.sem, v.at(f"full{t}"))
                    nc.scalar.activation(o, nfull[:, t % 3, :], ACT.Copy).then_inc(a.did(f"hi{t}"), 1)
                for t in range(KT if squares else 0):
                    act.wait_ge(v.sem, v.at(f"full{t}"))
                    if t >= 2:
                        act.wait_ge(v.sem, v.at(f"acc{t - 2}"))
                    nc.scalar.activation(nsq[:, t % 2, :], x[:, t, :], ACT.Square).then_inc(a.did(f"sq{t}"), 1)

            act.wait_ge(proV.sem, proV.at("sub1"))
            nc.scalar.activation(lb[:, 1:3, :], lb[:, 1:3, :], ACT.Exp).then_inc(proA.did("exp"), 1)
            act.wait_ge(ld_x, 16)
            for t in range(KT):
                if t >= 2:
                    act.wait_ge(proV.sem, proV.at(f"acc{t - 2}"))
                nc.scalar.activation(nsq[:, t % 2, :], x[:, t, :], ACT.Square).then_inc(proA.did(f"sq{t}"), 1)
                if t < LOOKAHEAD:
                    act.wait_ge(raw_loaded[t % 2], 16 * (t // 2 + 1))
                    nc.scalar.activation(whi[:, t, :], raw[:, t % 2, :], ACT.Copy).then_inc(hi_done, 1)
            norm(n0, [hhi[:, t, :] for t in range(KT)])

            with act.Fori(0, ROUNDS["v"] // 2) as i:
                for par in range(2):
                    r = 2 * i + par
                    for j in range(4):
                        cut(r, j)
                    used(r, 3)
                    for t in range(TT):
                        nc.scalar.activation(vraw[:, t, bass.ds(r * S, S)], bank[4 * par + t][:, :],
                                             ACT.Gelu_apprx_tanh).then_inc(vA.did(f"gelu{t}"), 1)
            act.wait_ge(vaV.sem, vaV.at("mask"))
            act.dma_start(wt[0:64, :, :], ws[0:64, 0:2, :]).then_inc(ld_wt, 16)
            act.dma_start(wt[64:P, :, 64:P], ws[64:P, 0:2, 64:P]).then_inc(ld_wt, 16)
            act.wait_ge(vaV.sem, vaV.at("inv"))
            nc.scalar.activation(rstd[:, 2, :], rstd[:, 1, :], ACT.Sqrt).then_inc(vaA.did("root"), 1)

            with act.Fori(0, ROUNDS["uz"]) as i:
                r = i + FIRST["uz"]
                cut(r, 0)
                act.wait_ge(uzV.sem, uzV.at("norm", i))
                act.wait_ge(uzP.sem, uzP.at("mix1", i - 1))
                nc.scalar.activation(vhi[:, :, :], vraw[:, :, bass.ds(i * 2 * P, 2 * P)],
                                     ACT.Copy).then_inc(uzA.did("vhi"), 1)
                act.wait_ge(ld_wt, 32 * i + 32)
                nc.scalar.activation(wthi[:, :, :], wt[:, :, :], ACT.Copy).then_inc(uzA.did("whi"), 1)
                cut(r, 1)
                act.wait_ge(uzV.sem, uzV.at("gate0", i - 1))
                nc.scalar.activation(ug[:, 0, :], bank[0][:, :], ACT.Gelu_apprx_tanh).then_inc(uzA.did("u0"), 1)
                act.wait_ge(uzV.sem, uzV.at("wlo", i))
                act.dma_start(wt[0:64, :, :], ws[0:64, bass.ds(2 * i + 2, 2), :]).then_inc(ld_wt, 16)
                act.dma_start(wt[64:P, :, 64:P], ws[64:P, bass.ds(2 * i + 2, 2), 64:P]).then_inc(ld_wt, 16)
                cut(r, 2)
                act.wait_ge(uzV.sem, uzV.at("gate1", i - 1))
                nc.scalar.activation(ug[:, 1, :], bank[1][:, :], ACT.Gelu_apprx_tanh).then_inc(uzA.did("u1"), 1)
                for q in range(2):
                    act.wait_ge(uzP.sem, uzP.at(f"mix{q}", i))
                    act.wait_ge(uzV.sem, uzV.at(f"ylo{q}", i - 1))
                    nc.scalar.activation(mt[:, q, :], bank[4 + q][:, :], ACT.Copy).then_inc(uzA.did(f"mixed{q}"), 1)
                cut(r, 3)
                nc.scalar.activation(sz[:, 0, :], bank[2][:, :], ACT.Silu).then_inc(uzA.did("z0"), 1)
                used(r, 3)
                nc.scalar.activation(sz[:, 1, :], bank[3][:, :], ACT.Silu).then_inc(uzA.did("z1"), 1)

            act.wait_ge(uzV.sem, uzV.all())
            act.dma_start(x[:, :, :], xt).then_inc(ld_x1, 16)
            with act.Fori(0, ROUNDS["w1"]) as i:
                r = i + FIRST["w1"]
                for q in range(2):
                    for j in ((0, 1, 2), (3,))[q]:
                        cut(r, j)
                    act.wait_ge(w1V.sem, w1V.at(f"x{q}", i))
                    nc.scalar.activation(nsq[:, q, :], x[:, bass.ds(2 * i + q, 1), :],
                                         ACT.Square).then_inc(w1A.did(f"sq{q}"), 1)
            norm(nb, [hhi[:, t, :] for t in range(KT)] + [yhi[:, KT + t, :] for t in range(KT)])

            def table(q, head):
                rows = rel_tab[bass.ds(head, 1), :, :].rearrange("a p c -> p (a c)")
                act.dma_start(tab[:, q, 0:S - BD], rows[:, 0:S - BD]).then_inc(ld_tab[q], 16)
                act.dma_start(tab[BD:P, q, S - BD:S], rows[BD:P, S - BD:S]).then_inc(ld_tab[q], 16)

            act.wait_ge(st_rel, 32)
            act.wait_ge(w1V.sem, w1V.all())
            table(0, 0)
            table(1, 1)
            with act.Fori(0, ROUNDS["at"]) as i:
                r = i + FIRST["at"]

                def exps(q):
                    act.wait_ge(atV.sem, atV.at(f"neg{q}", i))
                    for t in range(TT):
                        row = sc[:, q, QO[t]:QO[t] + QW[t]]
                        e = nc.scalar.activation(row, row, ACT.Exp, bias=sm[:, q, 1, t:t + 1],
                                                 accum_out=sm[:, q, 2, t:t + 1])
                    e.then_inc(atA.did(f"exp{q}"), 1)
                    table(q, 2 * i + 2 + q)

                def transposed(q):
                    act.wait_ge(atP.sem, atP.at(f"t{q}", i))
                    for b, c, n in ((7, 0, KW[0]), (0, KW[0], KW[1]), (1, KW[0] + KW[1], KW[2] + KW[3])):
                        e = nc.scalar.activation(phi[:, q, c:c + n], bank[b][:, 0:n], ACT.Copy)
                    e.then_inc(atA.did(f"phi{q}"), 1)

                cut(r, 0)
                used(r, 0)
                nc.scalar.activation(khi[:, :], bank[0][:, :], ACT.Copy).then_inc(atA.did("khi"), 1)
                cut(r, 1)
                used(r, 1)
                nc.scalar.activation(qhi[:, :], bank[1][:, :], ACT.Copy, scale=BD ** -0.5).then_inc(atA.did("qhi"), 1)
                cut(r, 2)
                exps(0)
                cut(r, 3)
                nc.scalar.activation(avf[:, :], bank[2][:, :], ACT.Copy).then_inc(atA.did("v"), 1)
                transposed(0)
                act.wait_ge(atP.sem, atP.at("vt", i))
                nc.scalar.activation(avhi[:, :, :], bank[2][:, :].rearrange("p (t v) -> p t v", v=P),
                                     ACT.Copy).then_inc(atA.did("vhi"), 1)
                exps(1)
                used(r, 3)
                nc.scalar.activation(az[:, :], bank[3][:, :], ACT.Exp, scale=-1.0).then_inc(atA.did("ez"), 1)
                transposed(1)

            def squares(a, v, first):
                for m in range(KT):
                    cut(first + m // 4, m % 4)
                    if m:
                        sq(a, v, m - 1)
                sq(a, v, KT - 1)

            def sq(a, v, m):
                act.wait_ge(v.sem, v.at(f"x{m}"))
                if m >= 2:
                    act.wait_ge(v.sem, v.at(f"acc{m - 2}"))
                nc.scalar.activation(nsq[:, m % 2, :], x[:, m, :], ACT.Square).then_inc(a.did(f"sq{m}"), 1)

            squares(w2A, w2V, FIRST["w2"])
            norm(nf, [], squares=True)
            act.dma_start(xs, x[:, :, :]).then_inc(st_x, 16)
            norm(n2, [hhi[:, t, :] for t in range(KT)])

            def hg_round(r, par, project, stage):
                s, spar, rr = r - 1, 1 - par, r + FIRST["hg"]

                if stage:
                    pass
                if project:
                    cut(rr, 0)
                    act.wait_ge(hpV.sem, hpV.at("z", r - 1))
                    used(rr, 0)
                    nc.scalar.activation(he[:, :], bank[0][:, :], ACT.Exp, scale=-1.0).then_inc(hpA.did("ef"), 1)
                if stage:
                    act.wait_ge(htP.sem, htP.at("vt", s))
                    nc.scalar.activation(hvv[0], bank[4][:, :], ACT.Copy).then_inc(htA.did("vhi"), 1)
                    act.wait_ge(htP.sem, htP.at("kt", s))
                    nc.scalar.activation(hko[0], bank[5][:, :], ACT.Copy).then_inc(htA.did("kohi"), 1)
                if project:
                    act.wait_ge(hpV.sem, hpV.at("k", r))
                    nc.scalar.activation(hf[:, :], hf[:, :], ACT.Ln).then_inc(hpA.did("log"), 1)
                if stage:
                    act.wait_ge(htV.sem, htV.at("s", s))
                    nc.scalar.activation(hshi[:, :], hs[:, :], ACT.Copy).then_inc(htA.did("shi"), 1)
                if project:
                    act.wait_ge(hpV.sem, hpV.at("b", r))
                    nc.scalar.activation(heb[:, :], hb[:, :], ACT.Exp).then_inc(hpA.did("eb"), 1)
                    nc.scalar.activation(hen[:, :], hb[:, :], ACT.Exp, scale=-1.0).then_inc(hpA.did("en"), 1)
                    act.wait_ge(hpV.sem, hpV.at("rest", r))
                    nc.scalar.activation(hd[:, :], hd[:, :], ACT.Exp).then_inc(hpA.did("ed"), 1)
                    cut(rr, 1)
                    used(rr, 1)
                    nc.scalar.activation(hq[:, :], bank[1][:, :], ACT.Exp, scale=-1.0).then_inc(hpA.did("eq"), 1)
                    cut(rr, 2)
                    act.wait_ge(hpV.sem, hpV.at("kin", r))
                    nc.scalar.activation(hkhi[:, :], hen[:, :], ACT.Copy).then_inc(hpA.did("khi"), 1)
                    nc.scalar.activation(hqin[0][:, par, :], hq[:, :], ACT.Copy).then_inc(hpA.did("qhi"), 1)
                if stage:
                    for b in range(4):
                        n = 4 if b < 3 else 3
                        act.wait_ge(htV.sem, htV.at(f"st{4 * b + n}", s))
                        nc.scalar.activation(hss[0][:, 4 * b + 1:4 * b + 1 + n, :], hst[:, b % 2, 0:n, :],
                                             ACT.Copy).then_inc(htA.did(f"sthi{b}"), 1)
                if project:
                    cut(rr, 3)
                    nc.scalar.activation(hv[:, :], bank[2][:, :], ACT.Copy).then_inc(hpA.did("v"), 1)
                    used(rr, 3)
                    nc.scalar.activation(he[:, :], bank[3][:, :], ACT.Exp, scale=-1.0).then_inc(hpA.did("ez"), 1)
                if stage:
                    act.wait_ge(htP.sem, htP.at("o", s))
                    act.wait_ge(hoV.sem, hoV.at("ylo", s - 1))
                    nc.scalar.activation(ho[:, 0, :], bank[4][:, :], ACT.Square).then_inc(htA.did("sq"), 1)
                    act.wait_ge(hoV.sem, hoV.at("inv", s))
                    nc.scalar.activation(ho[:, 1, :], ho[:, 1, :], ACT.Sqrt).then_inc(hoA.did("root"), 1)

            act.wait_ge(st_x, 16)
            act.wait_ge(n2[2].sem, n2[2].all())
            act.dma_start(hm[:, :, :], masks_hg).then_inc(ld_hm, 16)
            hg_round(0, 0, True, False)
            with act.Fori(0, (HH - 2) // 2) as i:
                hg_round(2 * i + 1, 1, True, True)
                hg_round(2 * i + 2, 0, True, True)
            hg_round(HH - 1, 1, True, True)
            hg_round(HH, 0, False, True)

            act.wait_ge(hoV.sem, hoV.all())
            act.dma_start(mm[:, :, :], masks_ml).then_inc(ld_mm, 16)
            for n in range(8):
                cut(FIRST["dn"] + n // 4, n % 4)
                if 1 <= n <= QL + KL:
                    nc.scalar.activation(dsq[:, n - 1, :], bank[n - 1][:, :],
                                         ACT.Square).then_inc(dnA.did(f"sq{n - 1}"), 1)
            for g, name in enumerate(("iq", "ik")):
                act.wait_ge(dnV.sem, dnV.at(name))
                nc.scalar.activation(dr[:, g, 0, :], dr[:, g, 1, :], ACT.Sqrt).then_inc(dnA.did(("rq", "rk")[g]), 1)
            for t in range(QL + KL):
                act.wait_ge(dnV.sem, dnV.at(f"full{t}"))
                nc.scalar.activation(lhi[:, t, :], dsq[:, t, :], ACT.Copy).then_inc(dnA.did(f"hi{t}"), 1)
            nc.scalar.activation(mkp[:, 0, :], mt1[:, 0, :], ACT.Copy).then_inc(dnA.did("kphi"), 1)

            act.wait_ge(dnV.sem, dnV.all())
            with act.Fori(0, MH // 4) as i:
                for g in range(4):
                    t_ = 4 * i + g
                    r3 = 3 * i + FIRST["ml"]
                    n0_, n1_, n2_ = [(r3 + n // 4, n % 4) for n in range(3 * g, 3 * g + 3)]
                    cut(*n0_)
                    used(*n0_)
                    nc.scalar.activation(mq[:, 0, :], bank[0][:, :], ACT.Copy).then_inc(mlA.did("qhi"), 1)
                    cut(*n1_)
                    used(*n1_)
                    nc.scalar.activation(mk[:, 0, :], bank[2][:, :], ACT.Copy).then_inc(mlA.did("khi"), 1)
                    nc.scalar.activation(mv2[:, 0, :], bank[3][:, :], ACT.Copy).then_inc(mlA.did("vhi"), 1)
                    act.wait_ge(mlV.sem, mlV.at("qp", t_))
                    nc.scalar.activation(mqp[:, 0, :], mt1[:, 0, :], ACT.Copy).then_inc(mlA.did("qphi"), 1)
                    cut(*n2_)
                    act.wait_ge(mlV.sem, mlV.at("neg", t_))
                    for t in range(TT):
                        row = msc[:, QO[t]:QO[t] + QW[t]]
                        e = nc.scalar.activation(row, row, ACT.Exp, bias=msm[:, 1, t:t + 1],
                                                 accum_out=msm[:, 2, t:t + 1])
                    e.then_inc(mlA.did("exp"), 1)
                    used(*n2_)
                    nc.scalar.activation(mz[:, :], bank[2][:, :], ACT.Exp, scale=-1.0).then_inc(mlA.did("ez"), 1)
                    act.wait_ge(mlP.sem, mlP.at("t", t_))
                    for b, c, n in ((7, 0, KW[0]), (0, KW[0], KW[1]), (1, KW[0] + KW[1], KW[2] + KW[3])):
                        e = nc.scalar.activation(mph[:, c:c + n], bank[b][:, 0:n], ACT.Copy)
                    e.then_inc(mlA.did("phi"), 1)

            act.wait_ge(mlV.sem, mlV.all())
            act.dma_start(x[:, :, :], xs).then_inc(ld_x3, 16)
            with act.Fori(0, ROUNDS["mg"]) as i:
                r = i + FIRST["mg"]
                cut(r, 0)
                cut(r, 1)
                act.wait_ge(mgV.sem, mgV.at("lo", i - 1))
                nc.scalar.activation(mga[:, 0, :], bank[0][:, :], ACT.Sigmoid,
                                     bias=col("gate", i)).then_inc(mgA.did("g0"), 1)
                cut(r, 2)
                nc.scalar.activation(mga[:, 1, :], bank[1][:, :], ACT.Sigmoid,
                                     bias=col("gate", i + KT)).then_inc(mgA.did("g1"), 1)
                cut(r, 3)

            act.wait_ge(mgV.sem, mgV.all())
            squares(w3A, w3V, FIRST["w3"])
            norm(n3, [])

        @block.vector
        def _(dve):
            V = nc.vector
            prime(dve, [uzV, w1V, atV, hpV, hoV, mlV, mgV])

            def used(r, j):
                dve.wait_ge(slab_used, 4 * r + j + 2)

            def norm(steps_, outs, gains, width=D, squares=False, whole=False):
                p, a, v = steps_
                dve.wait_ge(p.sem, p.at("ms"))
                V.tensor_scalar(nr[:, 0, :], bank[7][:, :], 1.0 / width, EPS, ALU.mult,
                                ALU.add).then_inc(v.did("mean"), 1)
                dve.wait_ge(v.sem, v.at("mean"))
                V.reciprocal(nr[:, 1, :], nr[:, 0, :]).then_inc(v.did("inv"), 1)
                dve.wait_ge(a.sem, a.at("root"))
                n = len(gains)
                for t in range(n + 1):
                    if t < n:
                        if not whole and t >= 3:
                            dve.wait_ge(v.sem, v.at(f"lo{t - 3}"))
                        o = x[:, t, :] if whole else nfull[:, t % 3, :]
                        V.scalar_tensor_tensor(o, x[:, t % KT, :], gains[t], nr[:, 0, :], ALU.mult,
                                               ALU.mult).then_inc(v.did(f"full{t}"), 1)
                    if t >= 1 and not whole:
                        dve.wait_ge(a.sem, a.at(f"hi{t - 1}"))
                        V.tensor_tensor(outs[1][t - 1], nfull[:, (t - 1) % 3, :], f32(outs[0][t - 1]),
                                        ALU.subtract).then_inc(v.did(f"lo{t - 1}"), 1)
                    if t >= 1 and squares:
                        dve.wait_ge(a.sem, a.at(f"sq{t - 1}"))
                        add_square(v, t - 1)

            def add_square(v, t, name="acc"):
                if t == 0:
                    V.tensor_copy(nacc[:, :], nsq[:, 0, :]).then_inc(v.did(f"{name}0"), 1)
                else:
                    dve.wait_ge(v.sem, v.at(f"{name}{t - 1}"))
                    V.tensor_tensor(nacc[:, :], nacc[:, :], nsq[:, t % 2, :], ALU.add).then_inc(v.did(f"{name}{t}"), 1)

            def cols(name, n, first=0):
                return [vec[:, VEC[name] + first + t:VEC[name] + first + t + 1] for t in range(n)]

            h_tiles = [[u[:, t, :] for t in range(KT)] for u in (hhi, hlo)]

            dve.wait_ge(ld_ws, 16)
            V.memset(wt_all[64:P, :, 0:64], 0.0).then_inc(proV.did("mask"), 1)
            V.memset(nacc[:, :], 0.0).then_inc(proV.did("zero"), 1)
            dve.wait_ge(ld_vec, 32)
            l0, l1 = (vec[:, VEC[n]:VEC[n] + HH] for n in ("lb0", "lb1"))
            V.tensor_tensor(lb[:, 0, :], l0, l1, ALU.max).then_inc(proV.did("max"), 1)
            dve.wait_ge(proV.sem, proV.at("max"))
            V.tensor_tensor(lb[:, 1, :], l0, lb[:, 0, :], ALU.subtract).then_inc(proV.did("sub0"), 1)
            V.tensor_tensor(lb[:, 2, :], l1, lb[:, 0, :], ALU.subtract).then_inc(proV.did("sub1"), 1)
            dve.wait_ge(proA.sem, proA.at("exp"))
            V.tensor_tensor(lb[:, 0, :], lb[:, 1, :], lb[:, 2, :], ALU.add).then_inc(proV.did("sum"), 1)
            dve.wait_ge(proV.sem, proV.at("sum"))
            V.reciprocal(lb[:, 0, :], lb[:, 0, :]).then_inc(proV.did("inv"), 1)
            dve.wait_ge(proV.sem, proV.at("inv"))
            V.tensor_tensor(lb[:, 2, :], lb[:, 1, :], lb[:, 0, :], ALU.mult).then_inc(proV.did("low"), 1)
            dve.wait_ge(proV.sem, proV.at("low"))
            V.tensor_scalar(lb[:, 3, :], lb[:, 2, :], -1.0, 1.0, ALU.mult, ALU.add).then_inc(proV.did("high"), 1)
            for t in range(KT):
                dve.wait_ge(proA.sem, proA.at(f"sq{t}"))
                add_square(proV, t)
            dve.wait_ge(proP.sem, proP.at("rowsum"))
            dve.wait_ge(ld_bs, 16)
            for n in range(AH):
                last = V.scalar_tensor_tensor(bb[:, n, :], bank[n // 4][:, (n % 4) * P:(n % 4 + 1) * P],
                                              cols("ln_b", 1, n)[0], bb[:, n, :], ALU.mult, ALU.add)
            last.then_inc(proV.did("bb"), 1)
            norm(n0, h_tiles, cols("a_g", KT))

            with dve.Fori(0, ROUNDS["v"] // 2) as i:
                for par in range(2):
                    r = 2 * i + par
                    for t in range(TT):
                        dve.wait_ge(vA.sem, vA.at(f"gelu{t}", r))
                        V.bn_stats(stats[:, t, bass.ds(r, 1), :],
                                   vraw[:, t, bass.ds(r * S, S)]).then_inc(vV.did(f"stats{t}"), 1)
            V.memset(wt[64:P, :, 0:64], 0.0).then_inc(vaV.did("mask"), 1)
            dve.wait_ge(vV.sem, vV.all())
            for t in range(TT):
                last = V.bn_aggr(mv[:, t, :], stats[:, t, :, :])
            last.then_inc(vaV.did("aggr"), 1)
            dve.wait_ge(vaV.sem, vaV.at("aggr"))
            V.tensor_scalar(rstd[:, 0, :], mv[:, :, 1], EPS, None, ALU.add).then_inc(vaV.did("eps"), 1)
            dve.wait_ge(vaV.sem, vaV.at("eps"))
            V.reciprocal(rstd[:, 1, :], rstd[:, 0, :]).then_inc(vaV.did("inv"), 1)
            dve.wait_ge(vaA.sem, vaA.at("root"))
            V.scalar_tensor_tensor(rstd[:, 3, :], mv[:, :, 0], -1.0, rstd[:, 2, :], ALU.mult,
                                   ALU.mult).then_inc(vaV.did("shift"), 1)

            dve.wait_ge(vaV.sem, vaV.at("shift"))
            with dve.Fori(0, ROUNDS["uz"]) as i:
                dve.wait_ge(uzV.sem, uzV.at("ylo1", i - 1))
                for t in range(TT):
                    part = vraw[:, t, bass.ds(i * 2 * P, 2 * P)]
                    last = V.tensor_scalar(part, part, rstd[:, 2, t:t + 1], rstd[:, 3, t:t + 1], ALU.mult, ALU.add)
                last.then_inc(uzV.did("norm"), 1)
                dve.wait_ge(uzV.sem, uzV.at("norm", i))
                dve.wait_ge(uzA.sem, uzA.at("vhi", i))
                V.tensor_tensor(vlo[:, :, :], vraw[:, :, bass.ds(i * 2 * P, 2 * P)], f32(vhi[:, :, :]),
                                ALU.subtract).then_inc(uzV.did("vlo"), 1)
                dve.wait_ge(uzA.sem, uzA.at("whi", i))
                V.tensor_tensor(wtlo[:, :, :], wt[:, :, :], f32(wthi[:, :, :]), ALU.subtract).then_inc(uzV.did("wlo"), 1)
                for q in range(2):
                    dve.wait_ge(uzP.sem, uzP.at(f"turn{q}", i))
                    V.scalar_tensor_tensor(mt[:, q, :].rearrange("p (t v) -> p t v", v=P),
                                           bank[6 + q][:, :].rearrange("p (t v) -> p t v", v=P),
                                           col("ln_g", 2 * i + q),
                                           bb[:, bass.ds(2 * i + q, 1), :].to_broadcast([P, TT, P]),
                                           ALU.mult, ALU.add).then_inc(uzV.did(f"affine{q}"), 1)
                    dve.wait_ge(uzV.sem, uzV.at(f"affine{q}", i))
                    dve.wait_ge(uzA.sem, uzA.at(f"u{q}", i))
                    V.tensor_tensor(mt[:, q, :], mt[:, q, :], ug[:, q, :], ALU.mult).then_inc(uzV.did(f"gate{q}"), 1)
                    dve.wait_ge(uzV.sem, uzV.at(f"gate{q}", i))
                    dve.wait_ge(uzA.sem, uzA.at(f"z{q}", i))
                    V.tensor_tensor(mt[:, q, :], mt[:, q, :], sz[:, q, :], ALU.mult).then_inc(uzV.did(f"y{q}"), 1)
                    dve.wait_ge(uzV.sem, uzV.at(f"y{q}", i))
                    yh = yhi[:, bass.ds(2 * i + q, 1), :]
                    V.tensor_copy(yh, mt[:, q:q + 1, :]).then_inc(uzV.did(f"yhi{q}"), 1)
                    dve.wait_ge(uzV.sem, uzV.at(f"yhi{q}", i))
                    V.tensor_tensor(ylo[:, bass.ds(2 * i + q, 1), :], mt[:, q:q + 1, :], f32(yh),
                                    ALU.subtract).then_inc(uzV.did(f"ylo{q}"), 1)

            dve.wait_ge(uzV.sem, uzV.all())
            V.memset(nacc[:, :], 0.0).then_inc(w1Z.did("zero"), 1)
            dve.wait_ge(w1Z.sem, w1Z.at("zero"))
            dve.wait_ge(ld_x1, 16)
            with dve.Fori(0, ROUNDS["w1"]) as i:
                r = i + FIRST["w1"]
                dve.wait_ge(w1V.sem, w1V.at("acc1", i - 1))
                for q in range(2):
                    used(r, 2 * q + 1)
                    xt_ = x[:, bass.ds(2 * i + q, 1), :]
                    V.tensor_tensor(xt_, xt_, bank[2 * q][:, :].rearrange("p (a s) -> p a s", a=1),
                                    ALU.add).then_inc(w1V.did(f"x{q}"), 1)
                    dve.wait_ge(w1A.sem, w1A.at(f"sq{q}", i))
                    dve.wait_ge(w1V.sem, w1V.at(f"x{q}", i))
                    V.tensor_tensor(nacc[:, :], nacc[:, :], nsq[:, q, :], ALU.add).then_inc(w1V.did(f"acc{q}"), 1)
            hb_tiles = [[u[:, KT + t, :] for t in range(KT)] for u in (yhi, ylo)]
            norm(nb, [h_tiles[0] + hb_tiles[0], h_tiles[1] + hb_tiles[1]], cols("kv_g", KT) + cols("b_g", KT))

            for q in range(2):
                last = V.memset(tab[0:BD, q, S - BD:S], NEG)
            last.then_inc(atM.did("mask"), 1)
            dve.wait_ge(atM.sem, atM.at("mask"))
            with dve.Fori(0, ROUNDS["at"]) as i:
                r = i + FIRST["at"]
                srow = [(5, QW[2]), (6, 0), (5, 0), (4, 0)]
                dve.wait_ge(atV.sem, atV.at("ylo", i - 1))

                def maxima(q):
                    dve.wait_ge(atP.sem, atP.at(f"s{q}", i))
                    dve.wait_ge(ld_tab[q], 32 * i + 32)
                    V.memset(carry[:, q:q + 1], 0.0)
                    for t, (b, c) in enumerate(srow):
                        last = V.tensor_tensor_reduce(sc[:, q, QO[t]:QO[t] + QW[t]], bank[b][:, c:c + QW[t]],
                                                      tab[:, q, S - QW[t]:S], 1.0, -3e38, ALU.add, ALU.max,
                                                      sm[:, q, 0, t:t + 1])
                    last.then_inc(atV.did(f"max{q}"), 1)
                    dve.wait_ge(atV.sem, atV.at(f"max{q}", i))
                    V.tensor_scalar(sm[:, q, 1, :], sm[:, q, 0, :], -1.0, None, ALU.mult).then_inc(atV.did(f"neg{q}"), 1)

                def probabilities(q):
                    dve.wait_ge(atA.sem, atA.at(f"exp{q}", i))
                    V.reciprocal(sm[:, q, 3, :], sm[:, q, 2, :]).then_inc(atV.did(f"inv{q}"), 1)
                    dve.wait_ge(atV.sem, atV.at(f"inv{q}", i))
                    for t in range(TT):
                        row = sc[:, q, QO[t]:QO[t] + QW[t]]
                        last = V.tensor_scalar(row, row, sm[:, q, 3, t:t + 1], None, ALU.mult)
                    last.then_inc(atV.did(f"p{q}"), 1)

                def transposed(q):
                    dve.wait_ge(atA.sem, atA.at(f"phi{q}", i))
                    for b, c, n in ((7, 0, KW[0]), (0, KW[0], KW[1]), (1, KW[0] + KW[1], KW[2] + KW[3])):
                        last = V.tensor_tensor(plo[:, q, c:c + n], bank[b][:, 0:n], f32(phi[:, q, c:c + n]),
                                               ALU.subtract)
                    last.then_inc(atV.did(f"plo{q}"), 1)

                dve.wait_ge(atA.sem, atA.at("khi", i))
                V.tensor_tensor(klo[:, :], bank[0][:, :], f32(khi[:, :]), ALU.subtract).then_inc(atV.did("klo"), 1)
                dve.wait_ge(atA.sem, atA.at("qhi", i))
                V.scalar_tensor_tensor(qlo[:, :], bank[1][:, :], BD ** -0.5, f32(qhi[:, :]), ALU.mult,
                                       ALU.subtract).then_inc(atV.did("qlo"), 1)
                maxima(0)
                probabilities(0)
                maxima(1)
                transposed(0)
                dve.wait_ge(atA.sem, atA.at("vhi", i))
                V.tensor_tensor(avlo[:, :, :], bank[2][:, :].rearrange("p (t v) -> p t v", v=P), f32(avhi[:, :, :]),
                                ALU.subtract).then_inc(atV.did("vlo"), 1)
                probabilities(1)
                dve.wait_ge(atA.sem, atA.at("ez", i))
                V.tensor_scalar(az[:, :], az[:, :], 1.0, None, ALU.add).then_inc(atV.did("z1p"), 1)
                dve.wait_ge(atV.sem, atV.at("z1p", i))
                V.reciprocal(az[:, :], az[:, :]).then_inc(atV.did("zinv"), 1)
                dve.wait_ge(atV.sem, atV.at("zinv", i))
                V.tensor_tensor(az[:, :], bank[3][:, :], az[:, :], ALU.mult).then_inc(atV.did("z"), 1)
                transposed(1)
                dve.wait_ge(atV.sem, atV.at("z", i))
                for q in range(2):
                    rows = slice(BD * q, BD * (q + 1))
                    dve.wait_ge(atP.sem, atP.at(f"o{q}", i))
                    V.tensor_tensor(ay[rows, :], bank[4 + q][rows, :], az[rows, :],
                                    ALU.mult).then_inc(atV.did(f"y{q}"), 1)
                dve.wait_ge(atV.sem, atV.at("y1", i))
                yh = yhi[:, bass.ds(i, 1), :]
                y1 = ay[:, :].rearrange("p (a s) -> p a s", a=1)
                V.tensor_copy(yh, y1).then_inc(atV.did("yhi"), 1)
                dve.wait_ge(atV.sem, atV.at("yhi", i))
                V.tensor_tensor(ylo[:, bass.ds(i, 1), :], y1, f32(yh), ALU.subtract).then_inc(atV.did("ylo"), 1)

            def residual(a, v, first):
                V.memset(nacc[:, :], 0.0).then_inc(v.did("zero"), 1)
                for m in range(KT):
                    used(first + m // 4, m % 4)
                    V.tensor_tensor(x[:, m, :], x[:, m, :], bank[m % 4][:, :], ALU.add).then_inc(v.did(f"x{m}"), 1)
                    dve.wait_ge(a.sem, a.at(f"sq{m}"))
                    add_square(v, m)

            residual(w2A, w2V, FIRST["w2"])
            norm(nf, None, cols("fin1", KT), squares=True, whole=True)
            dve.wait_ge(nf[2].sem, nf[2].all())
            norm(n2, h_tiles, cols("n2_g", KT))

            def hg_finish(s, par):
                dve.wait_ge(hoV.sem, hoV.at("ylo", s - 1))
                dve.wait_ge(htP.sem, htP.at("ms", s))
                V.tensor_scalar(ho[:, 1, :], bank[5][:, :], 1.0 / P, EPS, ALU.mult, ALU.add).then_inc(hoV.did("mean"), 1)
                dve.wait_ge(hoV.sem, hoV.at("mean", s))
                V.reciprocal(ho[:, 1, :], ho[:, 1, :]).then_inc(hoV.did("inv"), 1)
                dve.wait_ge(hoA.sem, hoA.at("root", s))
                V.scalar_tensor_tensor(ho[:, 0, :], bank[4][:, :], cols("hg_g", 1)[0], ho[:, 1, :], ALU.mult,
                                       ALU.mult).then_inc(hoV.did("norm"), 1)
                dve.wait_ge(hoV.sem, hoV.at("norm", s))
                V.tensor_tensor(ho[:, 0, :], ho[:, 0, :], hz[:, par, :], ALU.mult).then_inc(hoV.did("y"), 1)
                dve.wait_ge(hoV.sem, hoV.at("y", s))
                yh = yhi[:, bass.ds(s, 1), :]
                V.tensor_copy(yh, ho[:, 0:1, :]).then_inc(hoV.did("yhi"), 1)
                dve.wait_ge(hoV.sem, hoV.at("yhi", s))
                V.tensor_tensor(ylo[:, bass.ds(s, 1), :], ho[:, 0:1, :], f32(yh), ALU.subtract).then_inc(hoV.did("ylo"), 1)

            def hg_round(r, par, project, stage):
                s, rr = r - 1, r + FIRST["hg"]
                if project:
                    dve.wait_ge(hpV.sem, hpV.at("z", r - 1))
                    dve.wait_ge(hpA.sem, hpA.at("ef", r))
                    V.tensor_scalar(he[:, :], he[:, :], 1.0, None, ALU.add).then_inc(hpV.did("f1p"), 1)
                    dve.wait_ge(hpV.sem, hpV.at("f1p", r))
                    V.reciprocal(he[:, :], he[:, :]).then_inc(hpV.did("finv"), 1)
                    dve.wait_ge(hpV.sem, hpV.at("finv", r))
                    V.tensor_scalar(hf[:, :], he[:, :], lb[:, 3, bass.ds(r, 1)], lb[:, 2, bass.ds(r, 1)], ALU.mult,
                                    ALU.add).then_inc(hpV.did("f"), 1)
                    dve.wait_ge(hpV.sem, hpV.at("f", r))
                    V.tensor_scalar(hk[:, :], hf[:, :], -1.0, 1.0, ALU.mult, ALU.add).then_inc(hpV.did("k"), 1)
                if stage:
                    dve.wait_ge(htA.sem, htA.at("vhi", s))
                    V.tensor_tensor(hvv[1], bank[4][:, :], f32(hvv[0]), ALU.subtract).then_inc(htV.did("vlo"), 1)
                    dve.wait_ge(htA.sem, htA.at("kohi", s))
                    V.tensor_tensor(hko[1], bank[5][:, :], f32(hko[0]), ALU.subtract).then_inc(htV.did("kolo"), 1)
                    dve.wait_ge(htP.sem, htP.at("s", s))
                    V.memset(carry[:, 2:3], 0.0)
                    V.copy_predicated(hs[:, :], hm[:, 1, :].bitcast(U32), bank[6][:, :]).then_inc(htV.did("s"), 1)
                if project:
                    dve.wait_ge(hpA.sem, hpA.at("log", r))
                    V.tensor_tensor_scan(hb[:, :], hm[:, 0, :], hf[:, :], 0.0, ALU.mult,
                                         ALU.add).then_inc(hpV.did("b"), 1)
                    dve.wait_ge(hpV.sem, hpV.at("b", r))
                    b3 = hb[:, :].rearrange("p (n c) -> p n c", c=HC)
                    V.tensor_tensor(hd[:, :].rearrange("p (n c) -> p n c", c=HC),
                                    b3[:, :, HC - 1:HC].to_broadcast([P, NCH, HC]), b3,
                                    ALU.subtract).then_inc(hpV.did("rest"), 1)
                if stage:
                    dve.wait_ge(htA.sem, htA.at("shi", s))
                    V.tensor_tensor(hslo[:, :], hs[:, :], f32(hshi[:, :]), ALU.subtract).then_inc(htV.did("slo"), 1)
                if project:
                    dve.wait_ge(hpA.sem, hpA.at("eq", r))
                    V.tensor_scalar(hq[:, :], hq[:, :], 1.0, None, ALU.add).then_inc(hpV.did("q1p"), 1)
                    dve.wait_ge(hpV.sem, hpV.at("q1p", r))
                    V.reciprocal(hq[:, :], hq[:, :]).then_inc(hpV.did("qinv"), 1)
                    dve.wait_ge(hpV.sem, hpV.at("qinv", r))
                    V.tensor_tensor(hq[:, :], bank[1][:, :], hq[:, :], ALU.mult).then_inc(hpV.did("q"), 1)
                    dve.wait_ge(hpV.sem, hpV.at("q", r))
                    V.tensor_tensor(hq[:, :], hq[:, :], heb[:, :], ALU.mult).then_inc(hpV.did("qin"), 1)
                    V.tensor_tensor(hen[:, :], hk[:, :], hen[:, :], ALU.mult).then_inc(hpV.did("kin"), 1)
                    V.tensor_tensor(hd[:, :], hk[:, :], hd[:, :], ALU.mult).then_inc(hpV.did("kout"), 1)
                    dve.wait_ge(hpA.sem, hpA.at("khi", r))
                    V.tensor_tensor(hklo[:, :], hen[:, :], f32(hkhi[:, :]), ALU.subtract).then_inc(hpV.did("klo"), 1)
                    dve.wait_ge(hpA.sem, hpA.at("qhi", r))
                    V.tensor_tensor(hqin[1][:, par, :], hq[:, :], f32(hqin[0][:, par, :]),
                                    ALU.subtract).then_inc(hpV.did("qlo"), 1)
                if stage:
                    for n in range(1, NCH):
                        b, c = (n - 1) // 4, (n - 1) % 4
                        if n == 1:
                            dve.wait_ge(htP.sem, htP.at("u", s))
                            V.tensor_copy(hst[:, 0, 0, :], bank[4][:, 0:P]).then_inc(htV.did("st1"), 1)
                        else:
                            dve.wait_ge(htV.sem, htV.at(f"st{n - 1}", s))
                            V.scalar_tensor_tensor(hst[:, b % 2, c, :], hst[:, (n - 2) // 4 % 2, (n - 2) % 4, :],
                                                   hdec[:, n - 1:n], bank[4 + c][:, b * P:(b + 1) * P], ALU.mult,
                                                   ALU.add).then_inc(htV.did(f"st{n}"), 1)
                        if c == 3 or n == NCH - 1:
                            dve.wait_ge(htV.sem, htV.at(f"st{n}", s))
                            dve.wait_ge(htA.sem, htA.at(f"sthi{b}", s))
                            V.tensor_tensor(hss[1][:, 4 * b + 1:n + 1, :], hst[:, b % 2, 0:c + 1, :],
                                            f32(hss[0][:, 4 * b + 1:n + 1, :]),
                                            ALU.subtract).then_inc(htV.did(f"stlo{b}"), 1)
                if project:
                    if stage:
                        dve.wait_ge(htV.sem, htV.at("stlo3", s))
                    dve.wait_ge(hpA.sem, hpA.at("eb", r))
                    V.tensor_copy(hdec[:, :], heb[:, :].rearrange("p (n c) -> p n c", c=HC)[:, :, HC - 1]
                                  ).then_inc(hpV.did("dec"), 1)
                    dve.wait_ge(hpA.sem, hpA.at("ez", r))
                    V.tensor_scalar(he[:, :], he[:, :], 1.0, None, ALU.add).then_inc(hpV.did("z1p"), 1)
                    dve.wait_ge(hpV.sem, hpV.at("z1p", r))
                    V.reciprocal(he[:, :], he[:, :]).then_inc(hpV.did("zinv"), 1)
                    dve.wait_ge(hpV.sem, hpV.at("zinv", r))
                    V.tensor_tensor(hz[:, par, :], bank[3][:, :], he[:, :], ALU.mult).then_inc(hpV.did("z"), 1)
                if stage:
                    hg_finish(s, 1 - par)

            dve.wait_ge(n2[2].sem, n2[2].all())
            dve.wait_ge(n2[1].sem, n2[1].all())
            V.memset(hs[:, :], 0.0).then_inc(hzV.did("zero"), 1)
            dve.wait_ge(ld_hm, 16)
            dve.wait_ge(hzV.sem, hzV.at("zero"))
            hg_round(0, 0, True, False)
            with dve.Fori(0, (HH - 2) // 2) as i:
                hg_round(2 * i + 1, 1, True, True)
                hg_round(2 * i + 2, 0, True, True)
            hg_round(HH - 1, 1, True, True)
            hg_round(HH, 0, False, True)

            def rotate(steps_, src, names, r=0):
                V.tensor_tensor(mt1[:, 0, :], src[ROPE:P, :], mm[ROPE:P, 1, :], ALU.mult).then_inc(steps_.did(names[0]), 1)
                V.tensor_tensor(mt1[:, 1, :], src[0:ROPE, :], mm[0:ROPE, 1, :], ALU.mult).then_inc(steps_.did(names[1]), 1)
                dve.wait_ge(steps_.sem, steps_.at(names[1], r))
                V.tensor_tensor(mt1[:, 0, :], mt1[:, 0, :], mt1[:, 1, :], ALU.add).then_inc(steps_.did(names[2]), 1)

            dve.wait_ge(ld_mm, 16)
            used(FIRST["dn"] + 1, 1)
            rotate(dnV, bank[5], ("turn", "straight", "kp"))
            for g, (b, n, width) in enumerate([(6, "q", QL * P), (7, "k", KL * P)]):
                dve.wait_ge(dnP.sem, dnP.at("ms" + n))
                V.tensor_scalar(dr[:, g, 0, :], bank[b][:, :], 1.0 / width, EPS, ALU.mult,
                                ALU.add).then_inc(dnV.did("m" + n), 1)
                dve.wait_ge(dnV.sem, dnV.at("m" + n))
                V.reciprocal(dr[:, g, 1, :], dr[:, g, 0, :]).then_inc(dnV.did("i" + n), 1)
            gains = cols("qa_g", QL) + cols("kva_g", KL)
            for t in range(QL + KL):
                dve.wait_ge(dnA.sem, dnA.at("rq" if t < QL else "rk"))
                V.scalar_tensor_tensor(dsq[:, t, :], bank[t][:, :], gains[t], dr[:, t // QL, 0, :], ALU.mult,
                                       ALU.mult).then_inc(dnV.did(f"full{t}"), 1)
            for t in range(QL + KL):
                dve.wait_ge(dnV.sem, dnV.at(f"full{t}"))
                dve.wait_ge(dnA.sem, dnA.at(f"hi{t}"))
                V.tensor_tensor(llo[:, t, :], dsq[:, t, :], f32(lhi[:, t, :]), ALU.subtract).then_inc(dnV.did(f"lo{t}"), 1)
            dve.wait_ge(dnA.sem, dnA.at("kphi"))
            V.tensor_tensor(mkp[:, 1, :], mt1[:, 0, :], f32(mkp[:, 0, :]), ALU.subtract).then_inc(dnV.did("kplo"), 1)

            with dve.Fori(0, MH // 4) as i:
                for g in range(4):
                    t_ = 4 * i + g
                    r3 = 3 * i + FIRST["ml"]
                    dve.wait_ge(mlV.sem, mlV.at("ylo", t_ - 1))
                    used(r3 + 3 * g // 4, 3 * g % 4)
                    rotate(mlV, bank[1], ("turn", "straight", "qp"), t_)
                    for src, dst, a, n in ((bank[0], mq, "qhi", "qlo"), (bank[2], mk, "khi", "klo"),
                                           (bank[3], mv2, "vhi", "vlo")):
                        dve.wait_ge(mlA.sem, mlA.at(a, t_))
                        V.tensor_tensor(dst[:, 1, :], src[:, :], f32(dst[:, 0, :]), ALU.subtract).then_inc(mlV.did(n), 1)
                    dve.wait_ge(mlA.sem, mlA.at("qphi", t_))
                    V.tensor_tensor(mqp[:, 1, :], mt1[:, 0, :], f32(mqp[:, 0, :]), ALU.subtract).then_inc(mlV.did("qplo"), 1)
                    dve.wait_ge(mlP.sem, mlP.at("s", t_))
                    V.memset(carry[:, 3:4], 0.0)
                    for t, (b, c) in enumerate([(5, QW[2]), (6, 0), (5, 0), (4, 0)]):
                        last = V.tensor_tensor_reduce(msc[:, QO[t]:QO[t] + QW[t]], bank[b][:, c:c + QW[t]],
                                                      mm[:, 0, S - QW[t]:S], (NOPE + ROPE) ** -0.5, -3e38, ALU.add,
                                                      ALU.max, msm[:, 0, t:t + 1])
                    last.then_inc(mlV.did("max"), 1)
                    dve.wait_ge(mlV.sem, mlV.at("max", t_))
                    V.tensor_scalar(msm[:, 1, :], msm[:, 0, :], -1.0, None, ALU.mult).then_inc(mlV.did("neg"), 1)
                    dve.wait_ge(mlA.sem, mlA.at("exp", t_))
                    V.reciprocal(msm[:, 3, :], msm[:, 2, :]).then_inc(mlV.did("inv"), 1)
                    dve.wait_ge(mlV.sem, mlV.at("inv", t_))
                    for t in range(TT):
                        row = msc[:, QO[t]:QO[t] + QW[t]]
                        last = V.tensor_scalar(row, row, msm[:, 3, t:t + 1], None, ALU.mult)
                    last.then_inc(mlV.did("p"), 1)
                    dve.wait_ge(mlA.sem, mlA.at("ez", t_))
                    V.tensor_scalar(mz[:, :], mz[:, :], 1.0, None, ALU.add).then_inc(mlV.did("z1p"), 1)
                    dve.wait_ge(mlV.sem, mlV.at("z1p", t_))
                    V.reciprocal(mz[:, :], mz[:, :]).then_inc(mlV.did("zinv"), 1)
                    dve.wait_ge(mlV.sem, mlV.at("zinv", t_))
                    V.tensor_tensor(mz[:, :], bank[2][:, :], mz[:, :], ALU.mult).then_inc(mlV.did("z"), 1)
                    dve.wait_ge(mlA.sem, mlA.at("phi", t_))
                    for b, c, n in ((7, 0, KW[0]), (0, KW[0], KW[1]), (1, KW[0] + KW[1], KW[2] + KW[3])):
                        last = V.tensor_tensor(mpl[:, c:c + n], bank[b][:, 0:n], f32(mph[:, c:c + n]), ALU.subtract)
                    last.then_inc(mlV.did("plo"), 1)
                    dve.wait_ge(mlV.sem, mlV.at("z", t_))
                    dve.wait_ge(mlP.sem, mlP.at("o", t_))
                    V.tensor_tensor(my[:, :], bank[3][:, :], mz[:, :], ALU.mult).then_inc(mlV.did("y"), 1)
                    dve.wait_ge(mlV.sem, mlV.at("y", t_))
                    yh = yhi[:, bass.ds(t_ + KT, 1), :]
                    y1 = my[:, :].rearrange("p (a s) -> p a s", a=1)
                    V.tensor_copy(yh, y1).then_inc(mlV.did("yhi"), 1)
                    dve.wait_ge(mlV.sem, mlV.at("yhi", t_))
                    V.tensor_tensor(ylo[:, bass.ds(t_ + KT, 1), :], y1, f32(yh), ALU.subtract).then_inc(mlV.did("ylo"), 1)

            with dve.Fori(0, ROUNDS["mg"]) as i:
                r = i + FIRST["mg"]
                dve.wait_ge(mgV.sem, mgV.at("lo", i - 1))
                used(r, 2)
                dve.wait_ge(mgA.sem, mgA.at("g1", i))
                V.tensor_tensor(mga[:, 0, :], bank[2][:, :], mga[:, 0, :], ALU.mult).then_inc(mgV.did("a"), 1)
                used(r, 3)
                V.tensor_tensor(mga[:, 1, :], bank[3][:, :], mga[:, 1, :], ALU.mult).then_inc(mgV.did("b"), 1)
                dve.wait_ge(mgV.sem, mgV.at("b", i))
                V.tensor_tensor(mga[:, 0, :], mga[:, 0, :], mga[:, 1, :], ALU.add).then_inc(mgV.did("sum"), 1)
                dve.wait_ge(mgV.sem, mgV.at("sum", i))
                gh = mgh[:, bass.ds(i, 1), :]
                V.tensor_copy(gh, mga[:, 0:1, :]).then_inc(mgV.did("hi"), 1)
                dve.wait_ge(mgV.sem, mgV.at("hi", i))
                V.tensor_tensor(mgl[:, bass.ds(i, 1), :], mga[:, 0:1, :], f32(gh), ALU.subtract).then_inc(mgV.did("lo"), 1)

            dve.wait_ge(ld_x3, 16)
            residual(w3A, w3V, FIRST["w3"])
            norm(n3, None, cols("fin2", KT), whole=True)

        for s in all_steps:
            assert s.next % s.n == 0 and s.next, s.names


def _feature_slabs(wm):
    k, c = wm.shape
    a = wm.reshape(k // D, KT, P, c // P, P)
    return a.transpose(3, 0, 2, 1, 4).reshape(-1, P, SLAB)


def _token_slabs(wm):
    c = wm.shape[1]
    a = wm.reshape(4, 2, P, c // S, S)
    return a.transpose(3, 0, 2, 1, 4).reshape(-1, P, SLAB)


def _interleave(*lots):
    return np.stack(lots, axis=1).reshape(-1, P, SLAB)


def _pad(a, width=SLAB):
    return np.pad(a, [(0, 0)] * (a.ndim - 1) + [(0, width - a.shape[-1])])


def _weights(i):
    u, v, z = np.split(i["a_w_in"][0], 3, axis=1)
    us, zs = _feature_slabs(u), _feature_slabs(z)
    uz = np.concatenate([us.reshape(-1, 2, P, SLAB), zs.reshape(-1, 2, P, SLAB)], axis=1).reshape(-1, P, SLAB)
    k, va = np.split(i["w_kv"], 2, axis=1)
    q, za = np.split(i["b_w_qz"][0], 2, axis=1)
    at = _interleave(*(_feature_slabs(m) for m in (k, q, va, za)))
    wi = i["w_in_2"][0]
    cuts = np.cumsum([D, D, D, D, QL * P, KL * P, ROPE, D])
    hq, hf, hi, hz, cq, ckv, kr, mz, gl = np.split(wi, cuts, axis=1)
    hg = _interleave(*(_feature_slabs(m) for m in (hf, hq, hi, hz)))

    def swapped(m):
        return np.concatenate([m, m[..., ROPE // 2:], m[..., :ROPE // 2]], axis=-1)

    dn = np.concatenate([_feature_slabs(cq), _feature_slabs(ckv), _feature_slabs(swapped(kr)),
                         np.zeros((2, P, SLAB), wi.dtype)])
    uq = i["w_uq_2"][0].reshape(QL, P, MH, NOPE + ROPE)
    uq = np.concatenate([uq[..., :NOPE], swapped(uq[..., NOPE:])], axis=-1)
    uq = _pad(uq.transpose(2, 1, 0, 3).reshape(MH, P, -1))
    ukv = i["w_ukv_2"][0].reshape(KL, P, MH, 2 * P)
    ukv = _pad(ukv.transpose(2, 1, 0, 3).reshape(MH, P, -1))
    ml = _interleave(uq, ukv, _feature_slabs(mz))
    g0, g1 = np.split(gl, 2, axis=1)
    mg = _interleave(*(_feature_slabs(m) for m in (g0, g1, i["w_proj_a_2"][0], i["w_proj_b_2"][0])))
    parts = {"v": _token_slabs(v), "uz": uz, "w1": _feature_slabs(i["a_w_out"][0]), "at": at,
             "w2": _feature_slabs(i["b_w_out"][0]), "hg": hg, "dn": dn, "ml": ml, "mg": mg,
             "w3": _feature_slabs(i["w_out_2"][0])}
    for name, rounds in ROUNDS.items():
        assert parts[name].shape[0] == 4 * rounds, name
    return np.concatenate([parts[name] for name in ROUNDS])


def _tables():
    f = np.float32
    p, c = np.arange(P)[:, None], np.arange(S)[None, :]
    consts = np.concatenate([np.eye(P, dtype=f), np.ones((P, P), f)], axis=1)
    starts = np.broadcast_to(np.where(c % HC == 0, f(0), f(1)), (P, S))
    t = c % P
    causal = np.where((p // HC == t // HC) & (p <= t), f(1), f(0))
    later = np.where(c - (S - P) > p, f(NEG), f(0))
    inv = f(10000.0) ** (-np.arange(0, ROPE, 2, dtype=f) / f(ROPE))
    ang = np.arange(S, dtype=f)[None, :] * inv[:, None]
    cos, sin = np.cos(ang), np.sin(ang)
    turn = np.concatenate([cos, cos, -sin, sin])
    return consts, np.stack([starts, causal], axis=1).astype(f), np.stack([later, turn], axis=1).astype(f)


def kernel(**inputs):
    import concourse.bacc as _bacc
    from concourse.bass_utils import run_bass_kernel_spmd as _run

    i = {name: np.asarray(a) for name, a in inputs.items()}
    vecs = [i[n].reshape(-1, P).T for n in ("a_norm_g", "a_ln_g", "a_ln_b", "kv_norm_g", "b_norm_g",
                                            "final_norm_g", "norm_g_2", "b_gate_2")]
    vecs += [i["lb_logits_2"][0].reshape(-1, P).T, i["lb_logits_2"][1].reshape(-1, P).T]
    vecs += [i[n].reshape(-1, P).T for n in ("hg_norm_g_2", "q_a_g_2", "kv_a_g_2", "final_norm_g_2")]
    rel = i["b_rel_bias"][0][:, ::-1]
    consts, masks_hg, masks_ml = _tables()
    arrays = {
        "xt": i["x"][0].T.reshape(KT, P, S).transpose(1, 0, 2),
        "w": _weights(i),
        "vecs": np.concatenate(vecs, axis=1),
        "ws": np.pad(i["a_w_s"][0].transpose(2, 0, 1), ((0, 0), (0, 2), (0, 0))),
        "bs": i["a_b_s"][0],
        "relx": np.pad(rel, ((0, 0), (255, 0)), mode="edge")[:, :RELX],
        "consts": consts, "masks_hg": masks_hg, "masks_ml": masks_ml,
    }
    arrays = {n: np.ascontiguousarray(a) for n, a in arrays.items()}
    nc = _bacc.Bacc("TRN2", target_bir_lowering=False, num_devices=1)
    args = [nc.dram_tensor(n, a.shape, F32, kind="ExternalInput").ap() for n, a in arrays.items()]
    args.append(nc.dram_tensor("x_kept", (P, KT, S), F32, kind="Internal").ap())
    args.append(nc.dram_tensor("rel_tab", (BH + 2, P, S), F32, kind="Internal").ap())
    args.append(nc.dram_tensor("out", (KT, P, S), F32, kind="ExternalOutput").ap())
    build(nc, *args)
    r = _run(nc, [arrays], core_ids=[0])
    return np.asarray(r.results[0]["out"]).reshape(D, S).T.reshape(1, S, D)
```

```python
from contextlib import ExitStack

import numpy as np

import concourse.bass as bass
from concourse import mybir

F32 = mybir.dt.float32
F32R = mybir.dt.float32r
U32 = mybir.dt.uint32
ALU = mybir.AluOpType
ACT = mybir.ActivationFunctionType

P = 128
S = 512
D = 1024
KT = D // P
TT = S // P
AW = 2048
AH = AW // P
BH, BD = 16, 64
PAIRS = BH // 2
RELX = 640
HH = 8
HC = 32
NCH = S // HC
MH = 8
QL, KL = 3, 2
NOPE, ROPE = 128, 64
EPS = 1e-6
NEG = -1e30

SLAB = 1024
LOOKAHEAD = 3
OUT_STEPS = 6
ROUNDS = {"v": 4, "uz": 8, "w1": 4, "at": 8, "w2": 2, "hg": 8, "dn": 2, "ml": 8, "mg": 8, "w3": 2}
FIRST, _at = {}, 0
for _name, _rounds in ROUNDS.items():
    FIRST[_name] = _at
    _at += _rounds
NR = _at
NSLAB = 4 * NR
FULL, PAD = SLAB, 8
ML_WIDTHS = (QL * 2 * P, KL * 2 * P, FULL, PAD)
RUNS = [(0, FIRST["dn"] + 1, 4 * (FULL,)), (FIRST["dn"] + 1, 1, (FULL, FULL, PAD, PAD)),
        (FIRST["ml"], ROUNDS["ml"], ML_WIDTHS), (FIRST["mg"], NR - FIRST["mg"], 4 * (FULL,))]


def slab_width(n):
    return next(widths for first, count, widths in RUNS if first <= n // 4 < first + count)[n % 4]


VEC, _at = {}, 0
for _name, _cols in [("a_g", KT), ("ln_g", AH), ("ln_b", AH), ("kv_g", KT), ("b_g", KT), ("fin1", KT),
                     ("n2_g", KT), ("gate", 2 * KT), ("lb0", HH), ("lb1", HH), ("hg_g", 1), ("qa_g", QL),
                     ("kva_g", KL), ("fin2", KT)]:
    VEC[_name] = _at
    _at += _cols
NVEC = _at

QW = [P * (q + 1) for q in range(TT)]
QO = [sum(QW[:q]) for q in range(TT)]
SW = sum(QW)
KW = [S - P * k for k in range(TT)]
KO = [sum(KW[:k]) for k in range(TT)]


class Steps:

    def __init__(self, sem, names, rounds=1, prime=0):
        self.sem, self.names, self.rounds, self.prime = sem, list(names), rounds, prime
        self.n, self.next = len(self.names), 0
        assert len(set(self.names)) == self.n

    def did(self, name):
        assert self.names[self.next % self.n] == name, (name, self.names[self.next % self.n])
        self.next += 1
        return self.sem

    def at(self, name, r=0):
        return (r + self.prime) * self.n + (self.names.index(name) + 1)

    def all(self):
        return (self.rounds + self.prime) * self.n


def build(nc, xt, w, vecs, ws, bs, relx, consts, masks_hg, masks_ml, xs, rel_tab, out):
    ctx = ExitStack()
    with ctx:
        def sb(name, shape, dt, where=ctx):
            return where.enter_context(nc.sbuf_tensor(name, shape, dt))

        def sem(name):
            return ctx.enter_context(nc.semaphore(name))

        vec = sb("vec", [P, NVEC], F32)
        cst = sb("cst", [P, 2 * P + 1], F32)
        ident, ones, eps = cst[:, 0:P], cst[:, P:2 * P], cst[:, 2 * P:2 * P + 1]
        lb = sb("lb", [P, 4, HH], F32)
        carry = sb("carry", [P, 4], F32)
        raw = sb("raw", [P, 2, SLAB], F32)
        whi = sb("whi", [P, 4, SLAB], F32R)
        wlo = sb("wlo", [P, 4, SLAB], F32R)
        hhi = sb("hhi", [P, KT, S], F32R)
        hlo = sb("hlo", [P, KT, S], F32R)
        yhi = sb("yhi", [P, AH, S], F32R)
        ylo = sb("ylo", [P, AH, S], F32R)

        with ExitStack() as scope:
            x = sb("x", [P, KT, S], F32, scope)
            nsq = sb("nsq", [P, 2, S], F32, scope)
            nacc = sb("nacc", [P, S], F32, scope)
            nr = sb("nr", [P, 2, S], F32, scope)
            nfull = sb("nfull", [P, 3, S], F32, scope)
            bb = sb("bb", [P, AH, P], F32, scope)
            wt_all = sb("wt_all", [P, AH, P], F32, scope)
        with ExitStack() as scope:
            vraw = sb("vraw", [P, TT, AW], F32, scope)
            sb("room_bb", [P, AH, P], F32, scope)
            stats = sb("stats", [P, TT, 4, 6], F32, scope)
            mv = sb("mv", [P, TT, 2], F32, scope)
            rstd = sb("rstd", [P, 4, TT], F32, scope)
            vhi = sb("vhi", [P, TT, 2 * P], F32R, scope)
            vlo = sb("vlo", [P, TT, 2 * P], F32R, scope)
            wt = sb("wt", [P, 2, P], F32, scope)
            wthi = sb("wthi", [P, 2, P], F32R, scope)
            wtlo = sb("wtlo", [P, 2, P], F32R, scope)
            mt = sb("mt", [P, 2, S], F32, scope)
            ug = sb("ug", [P, 2, S], F32, scope)
            sz = sb("sz", [P, 2, S], F32, scope)
        with ExitStack() as scope:
            sb("room_x1", [P, KT, S], F32, scope)
            khi = sb("khi", [P, S], F32R, scope)
            klo = sb("klo", [P, S], F32R, scope)
            qhi = sb("qhi", [P, S], F32R, scope)
            qlo = sb("qlo", [P, S], F32R, scope)
            avhi = sb("avhi", [P, TT, P], F32R, scope)
            avlo = sb("avlo", [P, TT, P], F32R, scope)
            avf = sb("avf", [P, S], F32, scope)
            az = sb("az", [P, S], F32, scope)
            ay = sb("ay", [P, S], F32, scope)
            sc = sb("sc", [P, 2, SW], F32, scope)
            phi = sb("phi", [P, 2, SW], F32R, scope)
            plo = sb("plo", [P, 2, SW], F32R, scope)
            tab = sb("tab", [P, 2, S], F32, scope)
            sm = sb("sm", [P, 2, 4, TT], F32, scope)
        with ExitStack() as scope:
            he = sb("he", [P, S], F32, scope)
            hf = sb("hf", [P, S], F32, scope)
            hk = sb("hk", [P, S], F32, scope)
            hb = sb("hb", [P, S], F32, scope)
            hd = sb("hd", [P, S], F32, scope)
            heb = sb("heb", [P, S], F32, scope)
            hen = sb("hen", [P, S], F32, scope)
            hq = sb("hq", [P, S], F32, scope)
            hv = sb("hv", [P, S], F32, scope)
            hdec = sb("hdec", [P, 2, NCH], F32, scope)
            hkhi = sb("hkhi", [P, S], F32R, scope)
            hklo = sb("hklo", [P, S], F32R, scope)
            hs = sb("hs", [P, S], F32, scope)
            hshi = sb("hshi", [P, S], F32R, scope)
            hslo = sb("hslo", [P, S], F32R, scope)
            hst = sb("hst", [P, NCH, P], F32, scope)
            hz = sb("hz", [P, 2, S], F32, scope)
            ho = sb("ho", [P, 2, S], F32, scope)
            hm = sb("hm", [P, 2, S], F32, scope)
        hqin = [yhi[:, 8:10, :], ylo[:, 8:10, :]]
        hvv = [yhi[:, 10, :], ylo[:, 10, :]]
        hko = [yhi[:, 11, :], ylo[:, 11, :]]
        hss = [t[:, 12:16, :].rearrange("p a (b v) -> p (a b) v", v=P) for t in (yhi, ylo)]
        with ExitStack() as scope:
            lhi = sb("lhi", [P, QL + KL, S], F32R, scope)
            llo = sb("llo", [P, QL + KL, S], F32R, scope)
            mkp = sb("mkp", [ROPE, 2, S], F32R, scope)
            mm = sb("mm", [P, 2, S], F32, scope)
            mt1 = sb("mt1", [P, 2, S], F32, scope)
            with ExitStack() as part:
                dsq = sb("dsq", [P, QL + KL, S], F32, part)
                dr = sb("dr", [P, 2, 2, S], F32, part)
            with ExitStack() as part:
                mq = sb("mq", [P, 2, S], F32R, part)
                mqp = sb("mqp", [ROPE, 2, S], F32R, part)
                mk = sb("mk", [P, 2, S], F32R, part)
                mv2 = sb("mv2", [P, 2, 2, S], F32R, part)
                mz = sb("mz", [P, S], F32, part)
                msc = sb("msc", [P, SW], F32, part)
                mph = sb("mph", [P, SW], F32R, part)
                mpl = sb("mpl", [P, SW], F32R, part)
                msm = sb("msm", [P, 4, TT], F32, part)
        with ExitStack() as scope:
            sb("room_x2", [P, KT, S], F32, scope)
            mga = sb("mga", [P, 2, S], F32, scope)
            sb("room_n", [P, 6, S], F32, scope)
            mgh = sb("mgh", [P, KT, S], F32R, scope)
            mgl = sb("mgl", [P, KT, S], F32R, scope)

        bank = [ctx.enter_context(nc.psum_tensor(f"bank{i}", [P, S], F32)) for i in range(8)]

        raw_loaded = [sem("raw_loaded0"), sem("raw_loaded1")]
        hi_done = sem("hi_done")
        lo_done = sem("lo_done")
        slab_used = sem("slab_used")

        ld_vec, ld_x, ld_ws, ld_bs, ld_wt = sem("ld_vec"), sem("ld_x"), sem("ld_ws"), sem("ld_bs"), sem("ld_wt")
        ld_x1, ld_tab, ld_hm, ld_mm, ld_x3 = sem("ld_x1"), [sem("ld_tab0"), sem("ld_tab1")], sem("ld_hm"), sem("ld_mm"), sem("ld_x3")
        st_x, st_rel, st_out = sem("st_x"), sem("st_rel"), sem("st_out")

        all_steps = []

        def steps(name, names, rounds=1, prime=0):
            s = Steps(sem(name), names, rounds, prime)
            all_steps.append(s)
            return s

        def numbered(name, n):
            return [f"{name}{i}" for i in range(n)]

        proP = steps("pro_pe", ["rowsum"])
        proA = steps("pro_act", ["exp"] + numbered("sq", KT))
        proV = steps("pro_dve", ["mask", "zero", "max", "sub0", "sub1", "sum", "inv", "low", "high"]
                     + numbered("acc", KT) + ["bb"])

        def norm_steps(name, n, cut, squares=False):
            v = ["mean", "inv"]
            for t in range(n + 1):
                v += [f"full{t}"] if t < n else []
                if t >= 1:
                    v += [f"lo{t - 1}"] if cut else [f"acc{t - 1}"] if squares else []
            a = ["root"] + (numbered("hi", n) if cut else numbered("sq", n) if squares else [])
            return steps(name + "_pe", ["ms"]), steps(name + "_act", a), steps(name + "_dve", v)

        n0 = norm_steps("n0", KT, True)
        nb = norm_steps("nb", 2 * KT, True)
        nf = norm_steps("nf", KT, False, True)
        n2 = norm_steps("n2", KT, True)
        n3 = norm_steps("n3", KT, False)

        vA = steps("v_act", numbered("gelu", TT), ROUNDS["v"], prime=2)
        vV = steps("v_dve", numbered("stats", TT), ROUNDS["v"])
        vaA = steps("va_act", ["root"])
        vaV = steps("va_dve", ["mask", "aggr", "eps", "inv", "shift"])
        uzP = steps("uz_pe", ["mix0", "mix1", "turn0", "turn1"], ROUNDS["uz"], prime=1)
        uzA = steps("uz_act", ["vhi", "whi", "u0", "u1", "mixed0", "mixed1", "z0", "z1"], ROUNDS["uz"], prime=1)
        uzV = steps("uz_dve", ["norm", "vlo", "wlo"] + [f"{n}{q}" for q in range(2)
                    for n in ("affine", "gate", "y", "yhi", "ylo")], ROUNDS["uz"], prime=1)
        w1A = steps("w1_act", ["sq0", "sq1"], ROUNDS["w1"])
        w1V = steps("w1_dve", ["x0", "acc0", "x1", "acc1"], ROUNDS["w1"], prime=1)
        w1Z = steps("w1_zero", ["zero"])
        atP = steps("at_pe", ["s0", "s1", "t0", "vt"], ROUNDS["at"])
        atA = steps("at_act", ["khi", "qhi", "exp0", "v", "phi0", "vhi", "exp1", "z"], ROUNDS["at"], prime=1)
        atV = steps("at_dve", ["klo", "qlo", "max0", "neg0", "inv0", "p0", "max1", "neg1", "plo0", "vlo", "inv1",
                               "p1"], ROUNDS["at"], prime=1)
        auP = steps("au_pe", ["t1", "o0", "o1"], ROUNDS["at"])
        auA = steps("au_act", ["phi1"], ROUNDS["at"])
        auV = steps("au_dve", ["plo1", "y0", "y1", "yhi", "ylo"], ROUNDS["at"], prime=1)
        atM = steps("at_mask", ["mask"])
        w2A = steps("w2_act", numbered("sq", KT))
        w2V = steps("w2_dve", ["zero"] + [f"{n}{m}" for m in range(KT) for n in ("x", "acc")])
        hpA = steps("hp_act", ["q", "f", "log", "eb", "en", "ed", "v", "khi", "qhi"], HH, prime=1)
        hpV = steps("hp_dve", ["q", "f", "k", "b", "rest", "dec", "qin", "kin", "kout", "klo", "qlo"], HH, prime=1)
        htP = steps("ht_pe", ["vt", "kt", "s", "u", "o", "ms"], HH)
        htA = steps("ht_act", ["z", "vhi", "kohi", "shi"] + numbered("sthi", 4) + ["sq"], HH)
        htV = steps("ht_dve", ["vlo", "kolo", "s", "z", "slo"] + [f"st{n}" for n in range(1, 9)] + ["stlo0"]
                    + [f"st{n}" for n in range(9, 13)] + ["stlo1"] + [f"st{n}" for n in range(13, NCH)]
                    + ["stlo2", "stlo3"], HH, prime=1)
        hoA = steps("ho_act", ["ln", "root"], HH, prime=1)
        hoV = steps("ho_dve", ["norm", "y", "yhi", "ylo"], HH, prime=2)
        hzV = steps("hz_dve", ["zero"])
        dnP = steps("dn_pe", ["msq", "msk"])
        dnA = steps("dn_act", numbered("sq", QL + KL) + ["rq", "rk"] + numbered("hi", QL + KL) + ["kphi"])
        dnV = steps("dn_dve", ["turn", "straight", "kp", "mq", "iq", "mk", "ik"] + numbered("full", QL + KL)
                    + numbered("lo", QL + KL) + ["kplo"])
        mpP = steps("mp_pe", ["k", "s"], MH)
        mpA = steps("mp_act", ["qhi", "qphi", "khi", "vhi", "exp", "z"], MH, prime=1)
        mpV = steps("mp_dve", ["turn", "straight", "qp", "qlo", "qplo", "klo", "vlo", "max", "neg", "inv", "p"], MH,
                    prime=1)
        mtP = steps("mt_pe", ["t", "o"], MH)
        mtA = steps("mt_act", ["phi"], MH)
        mtV = steps("mt_dve", ["plo", "y", "yhi", "ylo"], MH, prime=1)
        mgA = steps("mg_act", ["g0", "g1"], ROUNDS["mg"], prime=1)
        mgV = steps("mg_dve", ["a", "b", "sum", "hi", "lo"], ROUNDS["mg"], prime=1)
        w3A = steps("w3_act", numbered("sq", KT))
        w3V = steps("w3_dve", ["zero"] + [f"{n}{m}" for m in range(KT) for n in ("x", "acc")])

        def prime(eng, those):
            for s in those:
                if s.prime:
                    eng.sem_inc(s.sem, s.prime * s.n)

        def col(name, i=0):
            return vec[:, bass.ds(VEC[name] + i, 1)]

        def f32(ap):
            return ap.bitcast(F32)

        block = ctx.enter_context(nc.Block())

        @block.sync
        def _(sp):
            def load(n, j, width):
                sp.dma_start(raw[:, j % 2, 0:width], w[n, :, 0:width]).then_inc(raw_loaded[j % 2], 16)

            load(0, 0, FULL)
            load(1, 1, FULL)
            for j in (2, 3):
                sp.wait_ge(lo_done, j - 1)
                load(j, j, FULL)
            for first, count, widths in RUNS:
                with sp.Fori(max(first, 1), first + count) as r:
                    for j in range(4):
                        sp.wait_ge(lo_done, 4 * r + j - 1)
                        load(4 * r + j, j, widths[j])
            for t in range(KT):
                sp.wait_ge(n3[2].sem, n3[2].at(f"full{t}"))
                sp.dma_start(out[t, :, :], x[:, t, :]).then_inc(st_out, 16)
            sp.wait_ge(st_out, 16 * KT)

        @block.gpsimd
        def _(pool):
            for first, count, widths in RUNS:
                with pool.Fori(first, first + count) as r:
                    for j in range(4):
                        width = widths[j]
                        pool.wait_ge(hi_done, 4 * r + j + 1)
                        nc.gpsimd.tensor_tensor(wlo[:, j, 0:width], raw[:, j % 2, 0:width],
                                                f32(whi[:, j, 0:width]), ALU.subtract).then_inc(lo_done, 1)

        @block.tensor
        def _(pe):
            pe.sem_inc(slab_used, 1)
            prime(pe, [uzP])

            def mm3(dst, a, b, first, last):
                nc.tensor.matmul(dst, a[0], b[0], start=first, stop=False)
                nc.tensor.matmul(dst, a[1], b[0], start=False, stop=False)
                return nc.tensor.matmul(dst, a[0], b[1], start=False, stop=last)

            def slab(r, j, dst, rhs, first=True, last=True, count=1, between=None):
                pe.wait_ge(lo_done, 4 * r + j + 1)
                for k in range(KT):
                    a = [t[:, j, k * P:(k + 1) * P] for t in (whi, wlo)]
                    b = [t[:, k, :] for t in rhs]
                    done = mm3(dst[:, :], a, b, first and k == 0, last and k == KT - 1)
                    if k == KT - 1:
                        done.then_inc(slab_used, count)
                    if between:
                        between(k)

            def norm(steps_, ready, value):
                pe.wait_ge(ready, value)
                nc.tensor.matmul(bank[7][:, :], ones, nacc[:, :], start=True,
                                 stop=True).then_inc(steps_[0].did("ms"), 1)

            h = (hhi, hlo)
            y_lower = (yhi[:, 0:KT, :], ylo[:, 0:KT, :])
            y_upper = (yhi[:, KT:AH, :], ylo[:, KT:AH, :])

            pe.wait_ge(ld_vec, 32)
            pe.wait_ge(proV.sem, proV.at("mask"))
            for i in range(4):
                rs = nc.tensor.matmul(bank[i][:, :], ones, wt_all[:, 4 * i:4 * i + 4, :], start=True, stop=True)
            rs.then_inc(proP.did("rowsum"), 1)
            norm(n0, proV.sem, proV.at(f"acc{KT - 1}"))
            pe.wait_ge(proV.sem, proV.all())

            with pe.Fori(0, ROUNDS["v"] // 2) as i:
                for par in range(2):
                    r = 2 * i + par
                    for j in range(4):
                        pe.wait_ge(lo_done, 4 * r + j + 1)
                        for k in (2 * j, 2 * j + 1):
                            pe.wait_ge(n0[2].sem, n0[2].at(f"lo{k}"))
                            for t in range(TT):
                                if k == 0:
                                    pe.wait_ge(vA.sem, vA.at(f"gelu{t}", r - 2))
                                a = [u[:, k, t * P:(t + 1) * P] for u in h]
                                b = [u[:, j, (k % 2) * S:(k % 2 + 1) * S] for u in (whi, wlo)]
                                done = mm3(bank[4 * par + t][:, :], a, b, k == 0, k == KT - 1)
                        done.then_inc(slab_used, 1)

            pe.wait_ge(vA.sem, vA.all())
            with pe.Fori(0, ROUNDS["uz"]) as i:
                r = i + FIRST["uz"]
                pe.wait_ge(uzA.sem, uzA.at("u0", i - 1))
                slab(r, 0, bank[0], h)
                pe.wait_ge(uzA.sem, uzA.at("u1", i - 1))
                slab(r, 1, bank[1], h)
                pe.wait_ge(uzV.sem, uzV.at("wlo", i))
                for q in range(2):
                    pe.wait_ge(uzA.sem, uzA.at(f"mixed{q}", i - 1))
                    cols = slice(q * P, (q + 1) * P)
                    mm3(bank[4 + q][:, :], (wthi[:, q, :], wtlo[:, q, :]), (vhi[:, :, cols], vlo[:, :, cols]),
                        True, True).then_inc(uzP.did(f"mix{q}"), 1)
                for q in range(2):
                    pe.wait_ge(uzA.sem, uzA.at(f"z{q}", i - 1))
                    slab(r, 2 + q, bank[2 + q], h)
                    pe.wait_ge(uzA.sem, uzA.at(f"mixed{q}", i))
                    pe.wait_ge(uzV.sem, uzV.at(f"affine{q}", i - 1))
                    for t in range(TT):
                        turn = nc.tensor.transpose(bank[6 + q][:, t * P:(t + 1) * P], mt[:, q, t * P:(t + 1) * P],
                                                   ident)
                    turn.then_inc(uzP.did(f"turn{q}"), 1)

            pe.wait_ge(uzV.sem, uzV.all())
            pe.wait_ge(uzA.sem, uzA.all())
            with pe.Fori(0, ROUNDS["w1"]) as i:
                r = i + FIRST["w1"]
                for q in range(2):
                    pe.wait_ge(w1V.sem, w1V.at(f"x{q}", i - 1))
                    slab(r, 2 * q, bank[2 * q], y_lower, last=False)
                    slab(r, 2 * q + 1, bank[2 * q], y_upper, first=False)
            norm(nb, w1V.sem, w1V.all())

            def at_scores(q):
                rows, base = slice(BD * q, BD * (q + 1)), 2 + 3 * q
                for t, (b, c) in enumerate([(1, QW[2]), (2, 0), (1, 0), (0, 0)]):
                    last = mm3(bank[base + b][:, c:c + QW[t]], [u[rows, t * P:(t + 1) * P] for u in (qhi, qlo)],
                               [u[rows, 0:QW[t]] for u in (khi, klo)], True, True)
                last.then_inc(atP.did(f"s{q}"), 1)

            def at_turned(q, steps_):
                for k in range(TT):
                    for t in range(k, TT):
                        b, c = [(0, 0), (1, 0), (2, 0), (2, KW[2])][k]
                        c += (t - k) * P
                        last = nc.tensor.transpose(bank[2 + 3 * q + b][:, c:c + P],
                                                   sc[:, q, QO[t] + k * P:QO[t] + (k + 1) * P], ident)
                last.then_inc(steps_.did(f"t{q}"), 1)

            def at_attended(q):
                for k in range(TT):
                    last = mm3(bank[5 + q][:, k * P:S], (avhi[:, k, :], avlo[:, k, :]),
                               [u[:, q, KO[k]:KO[k] + KW[k]] for u in (phi, plo)], k == 0, k == TT - 1)
                last.then_inc(auP.did(f"o{q}"), 1)

            def at_round(i, project, stage):
                r, s = i + FIRST["at"], i - 1
                if project:
                    pe.wait_ge(nb[2].sem, nb[2].at(f"lo{KT - 1}"))
                    pe.wait_ge(atV.sem, atV.at("vlo", i - 1))
                    slab(r, 0, bank[0], h)
                if stage:
                    pe.wait_ge(atV.sem, atV.at("p1", s))
                    at_turned(1, auP)
                if project:
                    pe.wait_ge(nb[2].sem, nb[2].all())
                    pe.wait_ge(atA.sem, atA.at("z", i - 1))
                    slab(r, 1, bank[1], y_upper)
                if stage:
                    pe.wait_ge(auV.sem, auV.at("plo1", s))
                    at_attended(0)
                    at_attended(1)
                if project:
                    pe.wait_ge(atV.sem, atV.at("qlo", i))
                    at_scores(0)
                    slab(r, 2, bank[0], h)
                    pe.wait_ge(auV.sem, auV.at("y1", s))
                    at_scores(1)
                    pe.wait_ge(atV.sem, atV.at("p0", i))
                    at_turned(0, atP)
                    pe.wait_ge(atA.sem, atA.at("v", i))
                    for t in range(TT):
                        last = nc.tensor.transpose(bank[0][:, t * P:(t + 1) * P], avf[:, t * P:(t + 1) * P], ident)
                    last.then_inc(atP.did("vt"), 1)
                    slab(r, 3, bank[1], y_upper)

            at_round(0, True, False)
            with pe.Fori(1, ROUNDS["at"]) as i:
                at_round(i, True, True)
            at_round(ROUNDS["at"], False, True)

            pe.wait_ge(auV.sem, auV.all())
            for m in range(KT):
                if m >= 4:
                    pe.wait_ge(w2V.sem, w2V.at(f"x{m - 4}"))
                slab(FIRST["w2"] + m // 4, m % 4, bank[m % 4], y_lower)
            norm(nf, w2V.sem, w2V.all())
            norm(n2, nf[2].sem, nf[2].all())

            def hg_project(r, name, between=None):
                j, b, st, read, n = {"q": (0, 0, hpV, "q", r - 1), "f": (1, 1, htV, "z", r - 1),
                                     "v": (2, 2, hpA, "v", r - 1), "z": (3, 1, hpA, "f", r)}[name]
                pe.wait_ge(st.sem, st.at(read, n))
                slab(r + FIRST["hg"], j, bank[b], h, between=between)

            def hg_turn(s, par, k):
                if k == 0:
                    pe.wait_ge(hpV.sem, hpV.at("qlo", s))
                    pe.wait_ge(hpA.sem, hpA.at("qhi", s))
                for n, src, name in ((0, hv, "vt"), (1, hd, "kt")):
                    if k == n:
                        for t in range(TT):
                            last = nc.tensor.transpose(bank[4 + n][:, t * P:(t + 1) * P], src[:, t * P:(t + 1) * P],
                                                       ident)
                        last.then_inc(htP.did(name), 1)
                if 2 <= k < 2 + TT:
                    cols = slice((k - 2) * P, (k - 1) * P)
                    last = mm3(bank[6][:, cols], (hkhi[:, cols], hklo[:, cols]),
                               [u[:, par, cols] for u in hqin], True, True)
                    if k == 1 + TT:
                        last.then_inc(htP.did("s"), 1)

            def hg_updates(s, k):
                if k == 0:
                    return
                if k == 1:
                    pe.wait_ge(htV.sem, htV.at("s", s))
                    pe.wait_ge(hoA.sem, hoA.at("ln", s - 1))
                n = NCH - 1
                for c in range((k - 1) * n // (KT - 1), k * n // (KT - 1)):
                    b, q = c // 4, c % 4
                    rows, cols = slice(HC * q, HC * (q + 1)), slice(b * P, (b + 1) * P)
                    last = mm3(bank[4 + q][:, b * P:(b + 1) * P], [u[rows, cols] for u in hko],
                               [u[rows, cols] for u in hvv], True, True)
                if k == KT - 1:
                    last.then_inc(htP.did("u"), 1)

            def hg_outputs(s, par, k):
                if k == 0:
                    pe.wait_ge(hoV.sem, hoV.at("norm", s - 1))
                if k >= OUT_STEPS:
                    return
                for half in range(k * 2 * TT // OUT_STEPS, (k + 1) * 2 * TT // OUT_STEPS):
                    b = half // 2
                    cols = slice(b * P, (b + 1) * P)
                    if half % 2 == 0:
                        pe.wait_ge(htV.sem, htV.at(f"stlo{b}", s))
                        mm3(bank[3][:, cols], [u[:, cols] for u in hvv], (hshi[:, cols], hslo[:, cols]), True,
                            False)
                    for n in range(max(1, 2 * half), 2 * half + 2):
                        c = slice(n * HC, (n + 1) * HC)
                        last = mm3(bank[3][:, c], [u[:, n, :] for u in hss], [u[:, par, c] for u in hqin], False,
                                   n == 4 * b + 3)
                if k == OUT_STEPS - 1:
                    last.then_inc(htP.did("o"), 1)

            def hg_square(s):
                pe.wait_ge(htA.sem, htA.at("sq", s))
                nc.tensor.matmul(bank[7][:, :], ones, ho[:, 0, :], start=True, stop=True).then_inc(htP.did("ms"), 1)

            def hg_round(r, par, project, stage):
                turn, updates, outputs = (lambda k: hg_turn(r - 1, 1 - par, k), lambda k: hg_updates(r - 1, k),
                                          lambda k: hg_outputs(r - 1, 1 - par, k))
                if not stage:
                    turn = updates = outputs = None
                if project:
                    hg_project(r, "q", turn)
                    hg_project(r, "f", updates)
                    hg_project(r, "v")
                    hg_project(r, "z", outputs)
                else:
                    for work in (turn, updates, outputs):
                        for k in range(KT):
                            work(k)
                if stage:
                    hg_square(r - 1)

            pe.wait_ge(n2[2].sem, n2[2].all())
            hg_round(0, 0, True, False)
            with pe.Fori(0, (HH - 2) // 2) as i:
                hg_round(2 * i + 1, 1, True, True)
                hg_round(2 * i + 2, 0, True, True)
            hg_round(HH - 1, 1, True, True)
            hg_round(HH, 0, False, True)

            pe.wait_ge(hoV.sem, hoV.all())
            for n in range(6):
                if n == 5:
                    pe.wait_ge(lo_done, 4 * FIRST["dn"] + 8)
                slab(FIRST["dn"] + n // 4, n % 4, bank[n], h, count=3 if n == 5 else 1)
            for g, (b, t0, n) in enumerate([(6, 0, QL), (7, QL, KL)]):
                for t in range(t0, t0 + n):
                    pe.wait_ge(dnA.sem, dnA.at(f"sq{t}"))
                    last = nc.tensor.matmul(bank[b][:, :], ones, dsq[:, t, :], start=t == t0, stop=t == t0 + n - 1)
                last.then_inc(dnP.did(("msq", "msk")[g]), 1)

            def ml_round(r, par, project, stage):
                rr, s = r + FIRST["ml"], r - 1
                if project:
                    pe.wait_ge(lo_done, 4 * rr + 1)
                    pe.wait_ge(mpV.sem, mpV.at("qlo", r - 1))
                    for b in range(2):
                        for k in range(QL):
                            c = (2 * k + b) * P
                            last = mm3(bank[b][:, :], [u[:, 0, c:c + P] for u in (whi, wlo)],
                                       (lhi[:, k, :], llo[:, k, :]), k == 0, k == QL - 1)
                    last.then_inc(slab_used, 1)
                if stage:
                    pe.wait_ge(mpV.sem, mpV.at("p", s))
                    for k in range(TT):
                        for t in range(k, TT):
                            b, c = [(4, 0), (5, 0), (6, 0), (6, KW[2])][k]
                            c += (t - k) * P
                            last = nc.tensor.transpose(bank[b][:, c:c + P],
                                                       msc[:, QO[t] + k * P:QO[t] + (k + 1) * P], ident)
                    last.then_inc(mtP.did("t"), 1)
                if project:
                    pe.wait_ge(lo_done, 4 * rr + 2)
                    pe.wait_ge(mpA.sem, mpA.at("z", r - 1))
                    for k in range(KL):
                        last = mm3(bank[2][:, :], [u[:, 1, 2 * k * P:(2 * k + 1) * P] for u in (whi, wlo)],
                                   (lhi[:, QL + k, :], llo[:, QL + k, :]), k == 0, k == KL - 1)
                    last.then_inc(mpP.did("k"), 1)
                    pe.wait_ge(mpV.sem, mpV.at("vlo", r - 1))
                    for t in range(TT):
                        cols = slice(t * P, (t + 1) * P)
                        for k in range(KL):
                            last = mm3(bank[3][:, cols], (lhi[:, QL + k, cols], llo[:, QL + k, cols]),
                                       [u[:, 1, (2 * k + 1) * P:(2 * k + 2) * P] for u in (whi, wlo)],
                                       k == 0, k == KL - 1)
                    last.then_inc(slab_used, 1)
                if stage:
                    pe.wait_ge(mtV.sem, mtV.at("plo", s))
                    for k in range(TT):
                        cols = slice(k * P, (k + 1) * P)
                        last = mm3(bank[7][:, k * P:S], (mv2[:, 1 - par, 0, cols], mv2[:, 1 - par, 1, cols]),
                                   [u[:, KO[k]:KO[k] + KW[k]] for u in (mph, mpl)], k == 0, k == TT - 1)
                    last.then_inc(mtP.did("o"), 1)
                if project:
                    pe.wait_ge(mpV.sem, mpV.at("klo", r))
                    for t, (b, c) in enumerate([(5, QW[2]), (6, 0), (5, 0), (4, 0)]):
                        cols = slice(t * P, (t + 1) * P)
                        mm3(bank[b][:, c:c + QW[t]], (mq[:, 0, cols], mq[:, 1, cols]),
                            (mk[:, 0, 0:QW[t]], mk[:, 1, 0:QW[t]]), True, False)
                        last = mm3(bank[b][:, c:c + QW[t]], (mqp[:, 0, cols], mqp[:, 1, cols]),
                                   (mkp[:, 0, 0:QW[t]], mkp[:, 1, 0:QW[t]]), False, True)
                    last.then_inc(mpP.did("s"), 1)
                    pe.wait_ge(lo_done, 4 * rr + 4)
                    slab(rr, 2, bank[2], h, count=2)

            pe.wait_ge(dnV.sem, dnV.all())
            ml_round(0, 0, True, False)
            with pe.Fori(0, (MH - 2) // 2) as i:
                ml_round(2 * i + 1, 1, True, True)
                ml_round(2 * i + 2, 0, True, True)
            ml_round(MH - 1, 1, True, True)
            ml_round(MH, 0, False, True)

            pe.wait_ge(mtV.sem, mtV.all())
            with pe.Fori(0, ROUNDS["mg"]) as i:
                r = i + FIRST["mg"]
                for j, (rhs, st, name) in enumerate([(h, mgA, "g0"), (h, mgA, "g1"), (y_lower, mgV, "a"),
                                                     (y_upper, mgV, "b")]):
                    pe.wait_ge(st.sem, st.at(name, i - 1))
                    slab(r, j, bank[j], rhs)

            pe.wait_ge(mgV.sem, mgV.all())
            for m in range(KT):
                if m >= 4:
                    pe.wait_ge(w3V.sem, w3V.at(f"x{m - 4}"))
                slab(FIRST["w3"] + m // 4, m % 4, bank[m % 4], (mgh, mgl))
            norm(n3, w3V.sem, w3V.all())

        @block.scalar
        def _(act):
            act.dma_start(vec[:, :], vecs).then_inc(ld_vec, 16)
            act.dma_start(cst[:, :], consts).then_inc(ld_vec, 16)
            act.dma_start(x[:, :, :], xt).then_inc(ld_x, 16)
            act.dma_start(wt_all[:, :, :], ws[:, 0:AH, :]).then_inc(ld_ws, 16)
            act.dma_start(bb[:, :, :], bs.partition_broadcast(P)).then_inc(ld_bs, 16)
            act.dma_start(rel_tab[0:BH, :, :], bass.AP(relx.tensor, P - 1,
                                                      [[RELX, BH], [-1, P], [1, S]])).then_inc(st_rel, 16)
            act.dma_start(rel_tab[BH:BH + 2, :, :], bass.AP(relx.tensor, P - 1,
                                                            [[RELX, 2], [-1, P], [1, S]])).then_inc(st_rel, 16)
            prime(act, [vA, uzA, mgA, hpA, hoA, mpA, atA])

            def cut(r, j, widths=4 * (FULL,)):
                slot = (j + LOOKAHEAD) % 4
                width = widths[slot]
                if isinstance(r, int):
                    if 4 * r + j + LOOKAHEAD >= NSLAB:
                        return
                    width = slab_width(4 * r + j + LOOKAHEAD)
                act.wait_ge(raw_loaded[slot % 2], 16 * (2 * r + (j + LOOKAHEAD) // 2 + 1))
                act.wait_ge(slab_used, 4 * r + j + 1)
                nc.scalar.activation(whi[:, slot, 0:width], raw[:, slot % 2, 0:width],
                                     ACT.Copy).then_inc(hi_done, 1)

            def used(r, j):
                act.wait_ge(slab_used, 4 * r + j + 2)

            def norm(steps_, outs, squares=False):
                _, a, v = steps_
                act.wait_ge(v.sem, v.at("inv"))
                nc.scalar.activation(nr[:, 0, :], nr[:, 1, :], ACT.Sqrt).then_inc(a.did("root"), 1)
                for t, o in enumerate(outs):
                    act.wait_ge(v.sem, v.at(f"full{t}"))
                    nc.scalar.activation(o, nfull[:, t % 3, :], ACT.Copy).then_inc(a.did(f"hi{t}"), 1)
                for t in range(KT if squares else 0):
                    act.wait_ge(v.sem, v.at(f"full{t}"))
                    if t >= 2:
                        act.wait_ge(v.sem, v.at(f"acc{t - 2}"))
                    nc.scalar.activation(nsq[:, t % 2, :], x[:, t, :], ACT.Square).then_inc(a.did(f"sq{t}"), 1)

            act.wait_ge(proV.sem, proV.at("sub1"))
            nc.scalar.activation(lb[:, 1:3, :], lb[:, 1:3, :], ACT.Exp).then_inc(proA.did("exp"), 1)
            act.wait_ge(ld_x, 16)
            for t in range(KT):
                if t >= 2:
                    act.wait_ge(proV.sem, proV.at(f"acc{t - 2}"))
                nc.scalar.activation(nsq[:, t % 2, :], x[:, t, :], ACT.Square).then_inc(proA.did(f"sq{t}"), 1)
                if t < LOOKAHEAD:
                    act.wait_ge(raw_loaded[t % 2], 16 * (t // 2 + 1))
                    nc.scalar.activation(whi[:, t, :], raw[:, t % 2, :], ACT.Copy).then_inc(hi_done, 1)
            norm(n0, [hhi[:, t, :] for t in range(KT)])

            with act.Fori(0, ROUNDS["v"] // 2) as i:
                for par in range(2):
                    r = 2 * i + par
                    for j in range(4):
                        cut(r, j)
                    used(r, 3)
                    for t in range(TT):
                        nc.scalar.activation(vraw[:, t, bass.ds(r * S, S)], bank[4 * par + t][:, :],
                                             ACT.Gelu_apprx_tanh).then_inc(vA.did(f"gelu{t}"), 1)
            act.wait_ge(vaV.sem, vaV.at("mask"))
            act.dma_start(wt[0:64, :, :], ws[0:64, 0:2, :]).then_inc(ld_wt, 16)
            act.dma_start(wt[64:P, :, 64:P], ws[64:P, 0:2, 64:P]).then_inc(ld_wt, 16)
            act.wait_ge(vaV.sem, vaV.at("inv"))
            nc.scalar.activation(rstd[:, 2, :], rstd[:, 1, :], ACT.Sqrt).then_inc(vaA.did("root"), 1)

            with act.Fori(0, ROUNDS["uz"]) as i:
                r = i + FIRST["uz"]
                cut(r, 0)
                act.wait_ge(uzV.sem, uzV.at("norm", i))
                act.wait_ge(uzP.sem, uzP.at("mix1", i - 1))
                nc.scalar.activation(vhi[:, :, :], vraw[:, :, bass.ds(i * 2 * P, 2 * P)],
                                     ACT.Copy).then_inc(uzA.did("vhi"), 1)
                act.wait_ge(ld_wt, 32 * i + 32)
                nc.scalar.activation(wthi[:, :, :], wt[:, :, :], ACT.Copy).then_inc(uzA.did("whi"), 1)
                cut(r, 1)
                act.wait_ge(uzV.sem, uzV.at("gate0", i - 1))
                nc.scalar.activation(ug[:, 0, :], bank[0][:, :], ACT.Gelu_apprx_tanh).then_inc(uzA.did("u0"), 1)
                act.wait_ge(uzV.sem, uzV.at("wlo", i))
                act.dma_start(wt[0:64, :, :], ws[0:64, bass.ds(2 * i + 2, 2), :]).then_inc(ld_wt, 16)
                act.dma_start(wt[64:P, :, 64:P], ws[64:P, bass.ds(2 * i + 2, 2), 64:P]).then_inc(ld_wt, 16)
                cut(r, 2)
                act.wait_ge(uzV.sem, uzV.at("gate1", i - 1))
                nc.scalar.activation(ug[:, 1, :], bank[1][:, :], ACT.Gelu_apprx_tanh).then_inc(uzA.did("u1"), 1)
                for q in range(2):
                    act.wait_ge(uzP.sem, uzP.at(f"mix{q}", i))
                    act.wait_ge(uzV.sem, uzV.at(f"ylo{q}", i - 1))
                    nc.scalar.activation(mt[:, q, :], bank[4 + q][:, :], ACT.Copy).then_inc(uzA.did(f"mixed{q}"), 1)
                cut(r, 3)
                nc.scalar.activation(sz[:, 0, :], bank[2][:, :], ACT.Silu).then_inc(uzA.did("z0"), 1)
                used(r, 3)
                nc.scalar.activation(sz[:, 1, :], bank[3][:, :], ACT.Silu).then_inc(uzA.did("z1"), 1)

            act.wait_ge(uzV.sem, uzV.all())
            act.dma_start(x[:, :, :], xt).then_inc(ld_x1, 16)
            with act.Fori(0, ROUNDS["w1"]) as i:
                r = i + FIRST["w1"]
                for q in range(2):
                    for j in ((0, 1, 2), (3,))[q]:
                        cut(r, j)
                    act.wait_ge(w1V.sem, w1V.at(f"x{q}", i))
                    nc.scalar.activation(nsq[:, q, :], x[:, bass.ds(2 * i + q, 1), :],
                                         ACT.Square).then_inc(w1A.did(f"sq{q}"), 1)
            norm(nb, [hhi[:, t, :] for t in range(KT)] + [yhi[:, KT + t, :] for t in range(KT)])

            def table(q, head):
                rows = rel_tab[bass.ds(head, 1), :, :].rearrange("a p c -> p (a c)")
                act.dma_start(tab[:, q, 0:S - BD], rows[:, 0:S - BD]).then_inc(ld_tab[q], 16)
                act.dma_start(tab[BD:P, q, S - BD:S], rows[BD:P, S - BD:S]).then_inc(ld_tab[q], 16)

            act.wait_ge(st_rel, 32)
            act.wait_ge(w1V.sem, w1V.all())
            table(0, 0)
            table(1, 1)

            def exps(i, q):
                act.wait_ge(atV.sem, atV.at(f"neg{q}", i))
                for t in range(TT):
                    row = sc[:, q, QO[t]:QO[t] + QW[t]]
                    e = nc.scalar.activation(row, row, ACT.Exp, bias=sm[:, q, 1, t:t + 1],
                                             accum_out=sm[:, q, 2, t:t + 1])
                e.then_inc(atA.did(f"exp{q}"), 1)
                table(q, 2 * i + 2 + q)

            def transposed(q, ready, done, i):
                act.wait_ge(ready.sem, ready.at(f"t{q}", i))
                for b, c, n in ((0, 0, KW[0]), (1, KW[0], KW[1]), (2, KW[0] + KW[1], KW[2] + KW[3])):
                    e = nc.scalar.activation(phi[:, q, c:c + n], bank[2 + 3 * q + b][:, 0:n], ACT.Copy)
                e.then_inc(done.did(f"phi{q}"), 1)

            def at_round(i, project, stage):
                r, s = i + FIRST["at"], i - 1
                if project:
                    cut(r, 0)
                    used(r, 0)
                    nc.scalar.activation(khi[:, :], bank[0][:, :], ACT.Copy).then_inc(atA.did("khi"), 1)
                if stage:
                    transposed(1, auP, auA, s)
                if project:
                    cut(r, 1)
                    used(r, 1)
                    nc.scalar.activation(qhi[:, :], bank[1][:, :], ACT.Copy, scale=BD ** -0.5).then_inc(atA.did("qhi"), 1)
                    cut(r, 2)
                    exps(i, 0)
                    used(r, 2)
                    nc.scalar.activation(avf[:, :], bank[0][:, :], ACT.Copy).then_inc(atA.did("v"), 1)
                    cut(r, 3)
                    act.wait_ge(auV.sem, auV.at("y1", s))
                    transposed(0, atP, atA, i)
                    act.wait_ge(atP.sem, atP.at("vt", i))
                    nc.scalar.activation(avhi[:, :, :], bank[0][:, :].rearrange("p (t v) -> p t v", v=P),
                                         ACT.Copy).then_inc(atA.did("vhi"), 1)
                    exps(i, 1)
                    act.preload_act_table_set("silu_and_others")
                    used(r, 3)
                    nc.scalar.activation(az[:, :], bank[1][:, :], ACT.Silu).then_inc(atA.did("z"), 1)
                    act.preload_act_table_set("exp_and_others")

            at_round(0, True, False)
            with act.Fori(1, ROUNDS["at"]) as i:
                at_round(i, True, True)
            at_round(ROUNDS["at"], False, True)

            def squares(a, v, first):
                for m in range(KT):
                    cut(first + m // 4, m % 4)
                    if m:
                        sq(a, v, m - 1)
                sq(a, v, KT - 1)

            def sq(a, v, m):
                act.wait_ge(v.sem, v.at(f"x{m}"))
                if m >= 2:
                    act.wait_ge(v.sem, v.at(f"acc{m - 2}"))
                nc.scalar.activation(nsq[:, m % 2, :], x[:, m, :], ACT.Square).then_inc(a.did(f"sq{m}"), 1)

            squares(w2A, w2V, FIRST["w2"])
            norm(nf, [], squares=True)
            act.dma_start(xs, x[:, :, :]).then_inc(st_x, 16)
            norm(n2, [hhi[:, t, :] for t in range(KT)])

            def states(s, b):
                first, last = 4 * b + 1, min(4 * b + 5, NCH)
                act.wait_ge(htV.sem, htV.at(f"st{last - 1}", s))
                nc.scalar.activation(hss[0][:, first:last, :], hst[:, first:last, :],
                                     ACT.Copy).then_inc(htA.did(f"sthi{b}"), 1)

            def hg_round(r, par, project, stage):
                s, spar, rr = r - 1, 1 - par, r + FIRST["hg"]
                if project:
                    cut(rr, 0)
                if stage:
                    used(rr - 1, 3)
                    act.wait_ge(hoV.sem, hoV.at("y", s - 2))
                    nc.scalar.activation(hz[:, spar, :], bank[1][:, :], ACT.Sigmoid).then_inc(htA.did("z"), 1)
                    act.wait_ge(htP.sem, htP.at("vt", s))
                    nc.scalar.activation(hvv[0], bank[4][:, :], ACT.Copy).then_inc(htA.did("vhi"), 1)
                    act.wait_ge(htP.sem, htP.at("kt", s))
                    nc.scalar.activation(hko[0], bank[5][:, :], ACT.Copy).then_inc(htA.did("kohi"), 1)
                    act.wait_ge(htV.sem, htV.at("s", s))
                    nc.scalar.activation(hshi[:, :], hs[:, :], ACT.Copy).then_inc(htA.did("shi"), 1)
                if project:
                    act.wait_ge(hpV.sem, hpV.at("qlo", r - 1))
                    used(rr, 0)
                    nc.scalar.activation(hq[:, :], bank[0][:, :], ACT.Sigmoid).then_inc(hpA.did("q"), 1)
                    cut(rr, 1)
                    used(rr, 1)
                    nc.scalar.activation(he[:, :], bank[1][:, :], ACT.Sigmoid).then_inc(hpA.did("f"), 1)
                    act.preload_act_table_set("natural_log_exp_and_others")
                if stage:
                    states(s, 0)
                if project:
                    act.wait_ge(hpV.sem, hpV.at("k", r))
                    nc.scalar.activation(hf[:, :], hf[:, :], ACT.Ln).then_inc(hpA.did("log"), 1)
                if stage:
                    states(s, 1)
                if project:
                    cut(rr, 2)
                    act.wait_ge(hpV.sem, hpV.at("b", r))
                    nc.scalar.activation(heb[:, :], hb[:, :], ACT.Exp).then_inc(hpA.did("eb"), 1)
                    nc.scalar.activation(hen[:, :], hb[:, :], ACT.Exp, scale=-1.0).then_inc(hpA.did("en"), 1)
                    act.wait_ge(hpV.sem, hpV.at("rest", r))
                    nc.scalar.activation(hd[:, :], hd[:, :], ACT.Exp).then_inc(hpA.did("ed"), 1)
                    used(rr, 2)
                    nc.scalar.activation(hv[:, :], bank[2][:, :], ACT.Copy).then_inc(hpA.did("v"), 1)
                if stage:
                    states(s, 2)
                    states(s, 3)
                if project:
                    cut(rr, 3)
                    act.wait_ge(hpV.sem, hpV.at("kin", r))
                    nc.scalar.activation(hkhi[:, :], hen[:, :], ACT.Copy).then_inc(hpA.did("khi"), 1)
                    nc.scalar.activation(hqin[0][:, par, :], hq[:, :], ACT.Copy).then_inc(hpA.did("qhi"), 1)
                else:
                    act.preload_act_table_set("natural_log_exp_and_others")
                if stage:
                    act.wait_ge(htP.sem, htP.at("o", s))
                    act.wait_ge(hoV.sem, hoV.at("ylo", s - 1))
                    nc.scalar.activation(ho[:, 0, :], bank[3][:, :], ACT.Square).then_inc(htA.did("sq"), 1)
                    act.wait_ge(htP.sem, htP.at("ms", s))
                    nc.scalar.activation(ho[:, 1, :], bank[7][:, :], ACT.Ln, bias=eps,
                                         scale=1.0 / P).then_inc(hoA.did("ln"), 1)
                    act.wait_ge(hoA.sem, hoA.at("ln", s))
                    nc.scalar.activation(ho[:, 1, :], ho[:, 1, :], ACT.Exp, scale=-0.5).then_inc(hoA.did("root"), 1)

            act.wait_ge(st_x, 16)
            act.wait_ge(n2[2].sem, n2[2].all())
            act.dma_start(hm[:, :, :], masks_hg).then_inc(ld_hm, 16)
            hg_round(0, 0, True, False)
            with act.Fori(0, (HH - 2) // 2) as i:
                hg_round(2 * i + 1, 1, True, True)
                hg_round(2 * i + 2, 0, True, True)
            hg_round(HH - 1, 1, True, True)
            hg_round(HH, 0, False, True)

            act.wait_ge(hoV.sem, hoV.all())
            act.dma_start(mm[:, :, :], masks_ml).then_inc(ld_mm, 16)
            for n in range(8):
                cut(FIRST["dn"] + n // 4, n % 4)
                if 1 <= n <= QL + KL:
                    nc.scalar.activation(dsq[:, n - 1, :], bank[n - 1][:, :],
                                         ACT.Square).then_inc(dnA.did(f"sq{n - 1}"), 1)
            for g, name in enumerate(("iq", "ik")):
                act.wait_ge(dnV.sem, dnV.at(name))
                nc.scalar.activation(dr[:, g, 0, :], dr[:, g, 1, :], ACT.Sqrt).then_inc(dnA.did(("rq", "rk")[g]), 1)
            for t in range(QL + KL):
                act.wait_ge(dnV.sem, dnV.at(f"full{t}"))
                nc.scalar.activation(lhi[:, t, :], dsq[:, t, :], ACT.Copy).then_inc(dnA.did(f"hi{t}"), 1)
            nc.scalar.activation(mkp[:, 0, :], mt1[0:ROPE, 0, :], ACT.Copy).then_inc(dnA.did("kphi"), 1)

            def ml_round(r, par, project, stage):
                rr, s = r + FIRST["ml"], r - 1
                if project:
                    cut(rr, 0, ML_WIDTHS)
                    used(rr, 0)
                    nc.scalar.activation(mq[:, 0, :], bank[0][:, :], ACT.Copy).then_inc(mpA.did("qhi"), 1)
                if stage:
                    act.wait_ge(mtP.sem, mtP.at("t", s))
                    act.wait_ge(mtV.sem, mtV.at("y", s - 1))
                    for b, c, n in ((4, 0, KW[0]), (5, KW[0], KW[1]), (6, KW[0] + KW[1], KW[2] + KW[3])):
                        e = nc.scalar.activation(mph[:, c:c + n], bank[b][:, 0:n], ACT.Copy)
                    e.then_inc(mtA.did("phi"), 1)
                if project:
                    act.wait_ge(mpV.sem, mpV.at("qp", r))
                    nc.scalar.activation(mqp[:, 0, :], mt1[0:ROPE, 0, :], ACT.Copy).then_inc(mpA.did("qphi"), 1)
                    act.wait_ge(mpP.sem, mpP.at("k", r))
                    nc.scalar.activation(mk[:, 0, :], bank[2][:, :], ACT.Copy).then_inc(mpA.did("khi"), 1)
                    cut(rr, 1, ML_WIDTHS)
                    used(rr, 1)
                    nc.scalar.activation(mv2[:, par, 0, :], bank[3][:, :], ACT.Copy).then_inc(mpA.did("vhi"), 1)
                    cut(rr, 2, ML_WIDTHS)
                    act.wait_ge(mpV.sem, mpV.at("neg", r))
                    for t in range(TT):
                        row = msc[:, QO[t]:QO[t] + QW[t]]
                        e = nc.scalar.activation(row, row, ACT.Exp, bias=msm[:, 1, t:t + 1],
                                                 accum_out=msm[:, 2, t:t + 1])
                    e.then_inc(mpA.did("exp"), 1)
                    act.preload_act_table_set("silu_and_others")
                    used(rr, 2)
                    act.wait_ge(mtV.sem, mtV.at("y", s))
                    nc.scalar.activation(mz[:, :], bank[2][:, :], ACT.Silu).then_inc(mpA.did("z"), 1)
                    act.preload_act_table_set("exp_and_others")
                    cut(rr, 3, ML_WIDTHS)

            act.wait_ge(dnV.sem, dnV.all())
            ml_round(0, 0, True, False)
            with act.Fori(0, (MH - 2) // 2) as i:
                ml_round(2 * i + 1, 1, True, True)
                ml_round(2 * i + 2, 0, True, True)
            ml_round(MH - 1, 1, True, True)
            ml_round(MH, 0, False, True)

            act.wait_ge(mtV.sem, mtV.all())
            act.dma_start(x[:, :, :], xs).then_inc(ld_x3, 16)
            with act.Fori(0, ROUNDS["mg"]) as i:
                r = i + FIRST["mg"]
                cut(r, 0)
                cut(r, 1)
                act.wait_ge(mgV.sem, mgV.at("lo", i - 1))
                nc.scalar.activation(mga[:, 0, :], bank[0][:, :], ACT.Sigmoid,
                                     bias=col("gate", i)).then_inc(mgA.did("g0"), 1)
                cut(r, 2)
                nc.scalar.activation(mga[:, 1, :], bank[1][:, :], ACT.Sigmoid,
                                     bias=col("gate", i + KT)).then_inc(mgA.did("g1"), 1)
                cut(r, 3)

            act.wait_ge(mgV.sem, mgV.all())
            squares(w3A, w3V, FIRST["w3"])
            norm(n3, [])

        @block.vector
        def _(dve):
            V = nc.vector
            prime(dve, [uzV, w1V, atV, auV, hpV, htV, hoV, mpV, mtV, mgV])

            def used(r, j):
                dve.wait_ge(slab_used, 4 * r + j + 2)

            def norm(steps_, outs, gains, width=D, squares=False, whole=False):
                p, a, v = steps_
                dve.wait_ge(p.sem, p.at("ms"))
                V.tensor_scalar(nr[:, 0, :], bank[7][:, :], 1.0 / width, EPS, ALU.mult,
                                ALU.add).then_inc(v.did("mean"), 1)
                dve.wait_ge(v.sem, v.at("mean"))
                V.reciprocal(nr[:, 1, :], nr[:, 0, :]).then_inc(v.did("inv"), 1)
                dve.wait_ge(a.sem, a.at("root"))
                n = len(gains)
                for t in range(n + 1):
                    if t < n:
                        if not whole and t >= 3:
                            dve.wait_ge(v.sem, v.at(f"lo{t - 3}"))
                        o = x[:, t, :] if whole else nfull[:, t % 3, :]
                        V.scalar_tensor_tensor(o, x[:, t % KT, :], gains[t], nr[:, 0, :], ALU.mult,
                                               ALU.mult).then_inc(v.did(f"full{t}"), 1)
                    if t >= 1 and not whole:
                        dve.wait_ge(a.sem, a.at(f"hi{t - 1}"))
                        V.tensor_tensor(outs[1][t - 1], nfull[:, (t - 1) % 3, :], f32(outs[0][t - 1]),
                                        ALU.subtract).then_inc(v.did(f"lo{t - 1}"), 1)
                    if t >= 1 and squares:
                        dve.wait_ge(a.sem, a.at(f"sq{t - 1}"))
                        add_square(v, t - 1)

            def add_square(v, t, name="acc"):
                if t == 0:
                    V.tensor_copy(nacc[:, :], nsq[:, 0, :]).then_inc(v.did(f"{name}0"), 1)
                else:
                    dve.wait_ge(v.sem, v.at(f"{name}{t - 1}"))
                    V.tensor_tensor(nacc[:, :], nacc[:, :], nsq[:, t % 2, :], ALU.add).then_inc(v.did(f"{name}{t}"), 1)

            def cols(name, n, first=0):
                return [vec[:, VEC[name] + first + t:VEC[name] + first + t + 1] for t in range(n)]

            h_tiles = [[u[:, t, :] for t in range(KT)] for u in (hhi, hlo)]

            dve.wait_ge(ld_ws, 16)
            V.memset(wt_all[64:P, :, 0:64], 0.0).then_inc(proV.did("mask"), 1)
            V.memset(nacc[:, :], 0.0).then_inc(proV.did("zero"), 1)
            dve.wait_ge(ld_vec, 32)
            l0, l1 = (vec[:, VEC[n]:VEC[n] + HH] for n in ("lb0", "lb1"))
            V.tensor_tensor(lb[:, 0, :], l0, l1, ALU.max).then_inc(proV.did("max"), 1)
            dve.wait_ge(proV.sem, proV.at("max"))
            V.tensor_tensor(lb[:, 1, :], l0, lb[:, 0, :], ALU.subtract).then_inc(proV.did("sub0"), 1)
            V.tensor_tensor(lb[:, 2, :], l1, lb[:, 0, :], ALU.subtract).then_inc(proV.did("sub1"), 1)
            dve.wait_ge(proA.sem, proA.at("exp"))
            V.tensor_tensor(lb[:, 0, :], lb[:, 1, :], lb[:, 2, :], ALU.add).then_inc(proV.did("sum"), 1)
            dve.wait_ge(proV.sem, proV.at("sum"))
            V.reciprocal(lb[:, 0, :], lb[:, 0, :]).then_inc(proV.did("inv"), 1)
            dve.wait_ge(proV.sem, proV.at("inv"))
            V.tensor_tensor(lb[:, 2, :], lb[:, 1, :], lb[:, 0, :], ALU.mult).then_inc(proV.did("low"), 1)
            dve.wait_ge(proV.sem, proV.at("low"))
            V.tensor_scalar(lb[:, 3, :], lb[:, 2, :], -1.0, 1.0, ALU.mult, ALU.add).then_inc(proV.did("high"), 1)
            for t in range(KT):
                dve.wait_ge(proA.sem, proA.at(f"sq{t}"))
                add_square(proV, t)
            dve.wait_ge(proP.sem, proP.at("rowsum"))
            dve.wait_ge(ld_bs, 16)
            for n in range(AH):
                last = V.scalar_tensor_tensor(bb[:, n, :], bank[n // 4][:, (n % 4) * P:(n % 4 + 1) * P],
                                              cols("ln_b", 1, n)[0], bb[:, n, :], ALU.mult, ALU.add)
            last.then_inc(proV.did("bb"), 1)
            norm(n0, h_tiles, cols("a_g", KT))

            with dve.Fori(0, ROUNDS["v"] // 2) as i:
                for par in range(2):
                    r = 2 * i + par
                    for t in range(TT):
                        dve.wait_ge(vA.sem, vA.at(f"gelu{t}", r))
                        V.bn_stats(stats[:, t, bass.ds(r, 1), :],
                                   vraw[:, t, bass.ds(r * S, S)]).then_inc(vV.did(f"stats{t}"), 1)
            V.memset(wt[64:P, :, 0:64], 0.0).then_inc(vaV.did("mask"), 1)
            dve.wait_ge(vV.sem, vV.all())
            for t in range(TT):
                last = V.bn_aggr(mv[:, t, :], stats[:, t, :, :])
            last.then_inc(vaV.did("aggr"), 1)
            dve.wait_ge(vaV.sem, vaV.at("aggr"))
            V.tensor_scalar(rstd[:, 0, :], mv[:, :, 1], EPS, None, ALU.add).then_inc(vaV.did("eps"), 1)
            dve.wait_ge(vaV.sem, vaV.at("eps"))
            V.reciprocal(rstd[:, 1, :], rstd[:, 0, :]).then_inc(vaV.did("inv"), 1)
            dve.wait_ge(vaA.sem, vaA.at("root"))
            V.scalar_tensor_tensor(rstd[:, 3, :], mv[:, :, 0], -1.0, rstd[:, 2, :], ALU.mult,
                                   ALU.mult).then_inc(vaV.did("shift"), 1)

            dve.wait_ge(vaV.sem, vaV.at("shift"))
            with dve.Fori(0, ROUNDS["uz"]) as i:
                dve.wait_ge(uzV.sem, uzV.at("ylo1", i - 1))
                for t in range(TT):
                    part = vraw[:, t, bass.ds(i * 2 * P, 2 * P)]
                    last = V.tensor_scalar(part, part, rstd[:, 2, t:t + 1], rstd[:, 3, t:t + 1], ALU.mult, ALU.add)
                last.then_inc(uzV.did("norm"), 1)
                dve.wait_ge(uzV.sem, uzV.at("norm", i))
                dve.wait_ge(uzA.sem, uzA.at("vhi", i))
                V.tensor_tensor(vlo[:, :, :], vraw[:, :, bass.ds(i * 2 * P, 2 * P)], f32(vhi[:, :, :]),
                                ALU.subtract).then_inc(uzV.did("vlo"), 1)
                dve.wait_ge(uzA.sem, uzA.at("whi", i))
                V.tensor_tensor(wtlo[:, :, :], wt[:, :, :], f32(wthi[:, :, :]), ALU.subtract).then_inc(uzV.did("wlo"), 1)
                for q in range(2):
                    dve.wait_ge(uzP.sem, uzP.at(f"turn{q}", i))
                    V.scalar_tensor_tensor(mt[:, q, :].rearrange("p (t v) -> p t v", v=P),
                                           bank[6 + q][:, :].rearrange("p (t v) -> p t v", v=P),
                                           col("ln_g", 2 * i + q),
                                           bb[:, bass.ds(2 * i + q, 1), :].to_broadcast([P, TT, P]),
                                           ALU.mult, ALU.add).then_inc(uzV.did(f"affine{q}"), 1)
                    dve.wait_ge(uzV.sem, uzV.at(f"affine{q}", i))
                    dve.wait_ge(uzA.sem, uzA.at(f"u{q}", i))
                    V.tensor_tensor(mt[:, q, :], mt[:, q, :], ug[:, q, :], ALU.mult).then_inc(uzV.did(f"gate{q}"), 1)
                    dve.wait_ge(uzV.sem, uzV.at(f"gate{q}", i))
                    dve.wait_ge(uzA.sem, uzA.at(f"z{q}", i))
                    V.tensor_tensor(mt[:, q, :], mt[:, q, :], sz[:, q, :], ALU.mult).then_inc(uzV.did(f"y{q}"), 1)
                    dve.wait_ge(uzV.sem, uzV.at(f"y{q}", i))
                    yh = yhi[:, bass.ds(2 * i + q, 1), :]
                    V.tensor_copy(yh, mt[:, q:q + 1, :]).then_inc(uzV.did(f"yhi{q}"), 1)
                    dve.wait_ge(uzV.sem, uzV.at(f"yhi{q}", i))
                    V.tensor_tensor(ylo[:, bass.ds(2 * i + q, 1), :], mt[:, q:q + 1, :], f32(yh),
                                    ALU.subtract).then_inc(uzV.did(f"ylo{q}"), 1)

            dve.wait_ge(uzV.sem, uzV.all())
            V.memset(nacc[:, :], 0.0).then_inc(w1Z.did("zero"), 1)
            dve.wait_ge(w1Z.sem, w1Z.at("zero"))
            dve.wait_ge(ld_x1, 16)
            with dve.Fori(0, ROUNDS["w1"]) as i:
                r = i + FIRST["w1"]
                dve.wait_ge(w1V.sem, w1V.at("acc1", i - 1))
                for q in range(2):
                    used(r, 2 * q + 1)
                    xt_ = x[:, bass.ds(2 * i + q, 1), :]
                    V.tensor_tensor(xt_, xt_, bank[2 * q][:, :].rearrange("p (a s) -> p a s", a=1),
                                    ALU.add).then_inc(w1V.did(f"x{q}"), 1)
                    dve.wait_ge(w1A.sem, w1A.at(f"sq{q}", i))
                    dve.wait_ge(w1V.sem, w1V.at(f"x{q}", i))
                    V.tensor_tensor(nacc[:, :], nacc[:, :], nsq[:, q, :], ALU.add).then_inc(w1V.did(f"acc{q}"), 1)
            hb_tiles = [[u[:, KT + t, :] for t in range(KT)] for u in (yhi, ylo)]
            norm(nb, [h_tiles[0] + hb_tiles[0], h_tiles[1] + hb_tiles[1]], cols("kv_g", KT) + cols("b_g", KT))

            for q in range(2):
                last = V.memset(tab[0:BD, q, S - BD:S], NEG)
            last.then_inc(atM.did("mask"), 1)
            dve.wait_ge(atM.sem, atM.at("mask"))

            def maxima(i, q):
                dve.wait_ge(atP.sem, atP.at(f"s{q}", i))
                dve.wait_ge(ld_tab[q], 32 * i + 32)
                V.memset(carry[:, q:q + 1], 0.0)
                for t, (b, c) in enumerate([(1, QW[2]), (2, 0), (1, 0), (0, 0)]):
                    last = V.tensor_tensor_reduce(sc[:, q, QO[t]:QO[t] + QW[t]], bank[2 + 3 * q + b][:, c:c + QW[t]],
                                                  tab[:, q, S - QW[t]:S], 1.0, -3e38, ALU.add, ALU.max,
                                                  sm[:, q, 0, t:t + 1])
                last.then_inc(atV.did(f"max{q}"), 1)
                dve.wait_ge(atV.sem, atV.at(f"max{q}", i))
                V.tensor_scalar(sm[:, q, 1, :], sm[:, q, 0, :], -1.0, None, ALU.mult).then_inc(atV.did(f"neg{q}"), 1)

            def probabilities(i, q):
                dve.wait_ge(atA.sem, atA.at(f"exp{q}", i))
                V.reciprocal(sm[:, q, 3, :], sm[:, q, 2, :]).then_inc(atV.did(f"inv{q}"), 1)
                dve.wait_ge(atV.sem, atV.at(f"inv{q}", i))
                for t in range(TT):
                    row = sc[:, q, QO[t]:QO[t] + QW[t]]
                    last = V.tensor_scalar(row, row, sm[:, q, 3, t:t + 1], None, ALU.mult)
                last.then_inc(atV.did(f"p{q}"), 1)

            def transposed(q, ready, done, i):
                dve.wait_ge(ready.sem, ready.at(f"phi{q}", i))
                for b, c, n in ((0, 0, KW[0]), (1, KW[0], KW[1]), (2, KW[0] + KW[1], KW[2] + KW[3])):
                    last = V.tensor_tensor(plo[:, q, c:c + n], bank[2 + 3 * q + b][:, 0:n], f32(phi[:, q, c:c + n]),
                                           ALU.subtract)
                last.then_inc(done.did(f"plo{q}"), 1)

            def at_round(i, project, stage):
                s = i - 1
                dve.wait_ge(atV.sem, atV.at("p1", i - 1))
                dve.wait_ge(auV.sem, auV.at("ylo", s - 1))
                if project:
                    dve.wait_ge(atA.sem, atA.at("khi", i))
                    V.tensor_tensor(klo[:, :], bank[0][:, :], f32(khi[:, :]), ALU.subtract).then_inc(atV.did("klo"), 1)
                if stage:
                    transposed(1, auA, auV, s)
                if project:
                    dve.wait_ge(atA.sem, atA.at("qhi", i))
                    V.scalar_tensor_tensor(qlo[:, :], bank[1][:, :], BD ** -0.5, f32(qhi[:, :]), ALU.mult,
                                           ALU.subtract).then_inc(atV.did("qlo"), 1)
                if stage:
                    dve.wait_ge(atA.sem, atA.at("z", s))
                    for q in range(2):
                        rows = slice(BD * q, BD * (q + 1))
                        dve.wait_ge(auP.sem, auP.at(f"o{q}", s))
                        V.tensor_tensor(ay[rows, :], bank[5 + q][rows, :], az[rows, :],
                                        ALU.mult).then_inc(auV.did(f"y{q}"), 1)
                    dve.wait_ge(auV.sem, auV.at("y1", s))
                    yh = yhi[:, bass.ds(s, 1), :]
                    y1 = ay[:, :].rearrange("p (a s) -> p a s", a=1)
                    V.tensor_copy(yh, y1).then_inc(auV.did("yhi"), 1)
                    dve.wait_ge(auV.sem, auV.at("yhi", s))
                    V.tensor_tensor(ylo[:, bass.ds(s, 1), :], y1, f32(yh), ALU.subtract).then_inc(auV.did("ylo"), 1)
                if project:
                    maxima(i, 0)
                    probabilities(i, 0)
                    maxima(i, 1)
                    transposed(0, atA, atV, i)
                    dve.wait_ge(atA.sem, atA.at("vhi", i))
                    V.tensor_tensor(avlo[:, :, :], bank[0][:, :].rearrange("p (t v) -> p t v", v=P), f32(avhi[:, :, :]),
                                    ALU.subtract).then_inc(atV.did("vlo"), 1)
                    probabilities(i, 1)

            at_round(0, True, False)
            with dve.Fori(1, ROUNDS["at"]) as i:
                at_round(i, True, True)
            at_round(ROUNDS["at"], False, True)

            def residual(a, v, first):
                V.memset(nacc[:, :], 0.0).then_inc(v.did("zero"), 1)
                for m in range(KT):
                    used(first + m // 4, m % 4)
                    V.tensor_tensor(x[:, m, :], x[:, m, :], bank[m % 4][:, :], ALU.add).then_inc(v.did(f"x{m}"), 1)
                    dve.wait_ge(a.sem, a.at(f"sq{m}"))
                    add_square(v, m)

            residual(w2A, w2V, FIRST["w2"])
            norm(nf, None, cols("fin1", KT), squares=True, whole=True)
            dve.wait_ge(nf[2].sem, nf[2].all())
            norm(n2, h_tiles, cols("n2_g", KT))

            def state(s, par, n):
                b, c = (n - 1) // 4, (n - 1) % 4
                if n == 1:
                    dve.wait_ge(htP.sem, htP.at("u", s))
                    V.tensor_copy(hst[:, 1, :], bank[4][:, 0:P]).then_inc(htV.did("st1"), 1)
                else:
                    dve.wait_ge(htV.sem, htV.at(f"st{n - 1}", s))
                    V.scalar_tensor_tensor(hst[:, n, :], hst[:, n - 1, :], hdec[:, par, n - 1:n],
                                           bank[4 + c][:, b * P:(b + 1) * P], ALU.mult,
                                           ALU.add).then_inc(htV.did(f"st{n}"), 1)

            def states_lo(s, b):
                first, last = 4 * b + 1, min(4 * b + 5, NCH)
                dve.wait_ge(htA.sem, htA.at(f"sthi{b}", s))
                V.tensor_tensor(hss[1][:, first:last, :], hst[:, first:last, :], f32(hss[0][:, first:last, :]),
                                ALU.subtract).then_inc(htV.did(f"stlo{b}"), 1)

            def hg_finish(s, par):
                dve.wait_ge(hoV.sem, hoV.at("ylo", s - 1))
                dve.wait_ge(hoA.sem, hoA.at("root", s))
                V.scalar_tensor_tensor(ho[:, 0, :], bank[3][:, :], cols("hg_g", 1)[0], ho[:, 1, :], ALU.mult,
                                       ALU.mult).then_inc(hoV.did("norm"), 1)
                dve.wait_ge(hoV.sem, hoV.at("norm", s))
                V.tensor_tensor(ho[:, 0, :], ho[:, 0, :], hz[:, par, :], ALU.mult).then_inc(hoV.did("y"), 1)
                dve.wait_ge(hoV.sem, hoV.at("y", s))
                yh = yhi[:, bass.ds(s, 1), :]
                V.tensor_copy(yh, ho[:, 0:1, :]).then_inc(hoV.did("yhi"), 1)
                dve.wait_ge(hoV.sem, hoV.at("yhi", s))
                V.tensor_tensor(ylo[:, bass.ds(s, 1), :], ho[:, 0:1, :], f32(yh), ALU.subtract).then_inc(hoV.did("ylo"), 1)

            def hg_round(r, par, project, stage):
                s, rr = r - 1, r + FIRST["hg"]
                if stage:
                    dve.wait_ge(htA.sem, htA.at("vhi", s))
                    V.tensor_tensor(hvv[1], bank[4][:, :], f32(hvv[0]), ALU.subtract).then_inc(htV.did("vlo"), 1)
                    dve.wait_ge(htA.sem, htA.at("kohi", s))
                    V.tensor_tensor(hko[1], bank[5][:, :], f32(hko[0]), ALU.subtract).then_inc(htV.did("kolo"), 1)
                    dve.wait_ge(htP.sem, htP.at("s", s))
                    V.memset(carry[:, 2:3], 0.0)
                    V.copy_predicated(hs[:, :], hm[:, 1, :].bitcast(U32), bank[6][:, :]).then_inc(htV.did("s"), 1)
                    V.tensor_tensor(hz[:, 1 - par, :], bank[1][:, :], hz[:, 1 - par, :], ALU.mult).then_inc(htV.did("z"), 1)
                    dve.wait_ge(htA.sem, htA.at("shi", s))
                    V.tensor_tensor(hslo[:, :], hs[:, :], f32(hshi[:, :]), ALU.subtract).then_inc(htV.did("slo"), 1)
                if project:
                    dve.wait_ge(hpA.sem, hpA.at("q", r))
                    V.tensor_tensor(hq[:, :], bank[0][:, :], hq[:, :], ALU.mult).then_inc(hpV.did("q"), 1)
                if stage:
                    for n in range(1, 5):
                        state(s, 1 - par, n)
                if project:
                    dve.wait_ge(hpA.sem, hpA.at("f", r))
                    V.tensor_scalar(hf[:, :], he[:, :], lb[:, 3, bass.ds(r, 1)], lb[:, 2, bass.ds(r, 1)], ALU.mult,
                                    ALU.add).then_inc(hpV.did("f"), 1)
                    dve.wait_ge(hpV.sem, hpV.at("f", r))
                    V.tensor_scalar(hk[:, :], hf[:, :], -1.0, 1.0, ALU.mult, ALU.add).then_inc(hpV.did("k"), 1)
                if stage:
                    for n in range(5, 9):
                        state(s, 1 - par, n)
                    states_lo(s, 0)
                if project:
                    dve.wait_ge(hpA.sem, hpA.at("log", r))
                    V.tensor_tensor_scan(hb[:, :], hm[:, 0, :], hf[:, :], 0.0, ALU.mult,
                                         ALU.add).then_inc(hpV.did("b"), 1)
                    dve.wait_ge(hpV.sem, hpV.at("b", r))
                    b3 = hb[:, :].rearrange("p (n c) -> p n c", c=HC)
                    V.tensor_tensor(hd[:, :].rearrange("p (n c) -> p n c", c=HC),
                                    b3[:, :, HC - 1:HC].to_broadcast([P, NCH, HC]), b3,
                                    ALU.subtract).then_inc(hpV.did("rest"), 1)
                if stage:
                    for n in range(9, 13):
                        state(s, 1 - par, n)
                    states_lo(s, 1)
                if project:
                    dve.wait_ge(hpA.sem, hpA.at("eb", r))
                    V.tensor_copy(hdec[:, par, :], heb[:, :].rearrange("p (n c) -> p n c", c=HC)[:, :, HC - 1]
                                  ).then_inc(hpV.did("dec"), 1)
                    V.tensor_tensor(hq[:, :], hq[:, :], heb[:, :], ALU.mult).then_inc(hpV.did("qin"), 1)
                if stage:
                    for n in range(13, NCH):
                        state(s, 1 - par, n)
                    states_lo(s, 2)
                if project:
                    dve.wait_ge(hpA.sem, hpA.at("en", r))
                    V.tensor_tensor(hen[:, :], hk[:, :], hen[:, :], ALU.mult).then_inc(hpV.did("kin"), 1)
                if stage:
                    states_lo(s, 3)
                if project:
                    dve.wait_ge(hpA.sem, hpA.at("ed", r))
                    V.tensor_tensor(hd[:, :], hk[:, :], hd[:, :], ALU.mult).then_inc(hpV.did("kout"), 1)
                    dve.wait_ge(hpA.sem, hpA.at("khi", r))
                    V.tensor_tensor(hklo[:, :], hen[:, :], f32(hkhi[:, :]), ALU.subtract).then_inc(hpV.did("klo"), 1)
                    dve.wait_ge(hpA.sem, hpA.at("qhi", r))
                    V.tensor_tensor(hqin[1][:, par, :], hq[:, :], f32(hqin[0][:, par, :]),
                                    ALU.subtract).then_inc(hpV.did("qlo"), 1)
                if stage:
                    hg_finish(s, 1 - par)

            dve.wait_ge(n2[2].sem, n2[2].all())
            dve.wait_ge(n2[1].sem, n2[1].all())
            V.memset(hs[:, :], 0.0).then_inc(hzV.did("zero"), 1)
            dve.wait_ge(ld_hm, 16)
            dve.wait_ge(hzV.sem, hzV.at("zero"))
            hg_round(0, 0, True, False)
            with dve.Fori(0, (HH - 2) // 2) as i:
                hg_round(2 * i + 1, 1, True, True)
                hg_round(2 * i + 2, 0, True, True)
            hg_round(HH - 1, 1, True, True)
            hg_round(HH, 0, False, True)

            def rotate(steps_, src, names, r=0):
                V.tensor_tensor(mt1[0:ROPE, 0, :], src[ROPE:P, :], mm[ROPE:P, 1, :], ALU.mult).then_inc(steps_.did(names[0]), 1)
                V.tensor_tensor(mt1[0:ROPE, 1, :], src[0:ROPE, :], mm[0:ROPE, 1, :], ALU.mult).then_inc(steps_.did(names[1]), 1)
                dve.wait_ge(steps_.sem, steps_.at(names[1], r))
                V.tensor_tensor(mt1[0:ROPE, 0, :], mt1[0:ROPE, 0, :], mt1[0:ROPE, 1, :], ALU.add).then_inc(steps_.did(names[2]), 1)

            dve.wait_ge(ld_mm, 16)
            used(FIRST["dn"] + 1, 1)
            rotate(dnV, bank[5], ("turn", "straight", "kp"))
            for g, (b, n, width) in enumerate([(6, "q", QL * P), (7, "k", KL * P)]):
                dve.wait_ge(dnP.sem, dnP.at("ms" + n))
                V.tensor_scalar(dr[:, g, 0, :], bank[b][:, :], 1.0 / width, EPS, ALU.mult,
                                ALU.add).then_inc(dnV.did("m" + n), 1)
                dve.wait_ge(dnV.sem, dnV.at("m" + n))
                V.reciprocal(dr[:, g, 1, :], dr[:, g, 0, :]).then_inc(dnV.did("i" + n), 1)
            gains = cols("qa_g", QL) + cols("kva_g", KL)
            for t in range(QL + KL):
                dve.wait_ge(dnA.sem, dnA.at("rq" if t < QL else "rk"))
                V.scalar_tensor_tensor(dsq[:, t, :], bank[t][:, :], gains[t], dr[:, t // QL, 0, :], ALU.mult,
                                       ALU.mult).then_inc(dnV.did(f"full{t}"), 1)
            for t in range(QL + KL):
                dve.wait_ge(dnV.sem, dnV.at(f"full{t}"))
                dve.wait_ge(dnA.sem, dnA.at(f"hi{t}"))
                V.tensor_tensor(llo[:, t, :], dsq[:, t, :], f32(lhi[:, t, :]), ALU.subtract).then_inc(dnV.did(f"lo{t}"), 1)
            dve.wait_ge(dnA.sem, dnA.at("kphi"))
            V.tensor_tensor(mkp[:, 1, :], mt1[0:ROPE, 0, :], f32(mkp[:, 0, :]), ALU.subtract).then_inc(dnV.did("kplo"), 1)

            def ml_round(r, par, project, stage):
                rr, s = r + FIRST["ml"], r - 1
                dve.wait_ge(mpV.sem, mpV.at("p", r - 1))
                dve.wait_ge(mtV.sem, mtV.at("ylo", s - 1))
                if project:
                    used(rr, 0)
                    rotate(mpV, bank[1], ("turn", "straight", "qp"), r)
                    dve.wait_ge(mpA.sem, mpA.at("qhi", r))
                    V.tensor_tensor(mq[:, 1, :], bank[0][:, :], f32(mq[:, 0, :]), ALU.subtract).then_inc(mpV.did("qlo"), 1)
                if stage:
                    dve.wait_ge(mtA.sem, mtA.at("phi", s))
                    for b, c, n in ((4, 0, KW[0]), (5, KW[0], KW[1]), (6, KW[0] + KW[1], KW[2] + KW[3])):
                        last = V.tensor_tensor(mpl[:, c:c + n], bank[b][:, 0:n], f32(mph[:, c:c + n]), ALU.subtract)
                    last.then_inc(mtV.did("plo"), 1)
                if project:
                    dve.wait_ge(mpA.sem, mpA.at("qphi", r))
                    V.tensor_tensor(mqp[:, 1, :], mt1[0:ROPE, 0, :], f32(mqp[:, 0, :]), ALU.subtract).then_inc(mpV.did("qplo"), 1)
                    dve.wait_ge(mpA.sem, mpA.at("khi", r))
                    V.tensor_tensor(mk[:, 1, :], bank[2][:, :], f32(mk[:, 0, :]), ALU.subtract).then_inc(mpV.did("klo"), 1)
                    dve.wait_ge(mpA.sem, mpA.at("vhi", r))
                    V.tensor_tensor(mv2[:, par, 1, :], bank[3][:, :], f32(mv2[:, par, 0, :]),
                                    ALU.subtract).then_inc(mpV.did("vlo"), 1)
                if stage:
                    dve.wait_ge(mpA.sem, mpA.at("z", s))
                    dve.wait_ge(mtP.sem, mtP.at("o", s))
                    V.tensor_tensor(mt1[:, 1, :], bank[7][:, :], mz[:, :], ALU.mult).then_inc(mtV.did("y"), 1)
                    dve.wait_ge(mtV.sem, mtV.at("y", s))
                    yh = yhi[:, bass.ds(s + KT, 1), :]
                    y1 = mt1[:, 1:2, :]
                    V.tensor_copy(yh, y1).then_inc(mtV.did("yhi"), 1)
                    dve.wait_ge(mtV.sem, mtV.at("yhi", s))
                    V.tensor_tensor(ylo[:, bass.ds(s + KT, 1), :], y1, f32(yh), ALU.subtract).then_inc(mtV.did("ylo"), 1)
                if project:
                    dve.wait_ge(mpP.sem, mpP.at("s", r))
                    V.memset(carry[:, 3:4], 0.0)
                    for t, (b, c) in enumerate([(5, QW[2]), (6, 0), (5, 0), (4, 0)]):
                        last = V.tensor_tensor_reduce(msc[:, QO[t]:QO[t] + QW[t]], bank[b][:, c:c + QW[t]],
                                                      mm[:, 0, S - QW[t]:S], (NOPE + ROPE) ** -0.5, -3e38, ALU.add,
                                                      ALU.max, msm[:, 0, t:t + 1])
                    last.then_inc(mpV.did("max"), 1)
                    dve.wait_ge(mpV.sem, mpV.at("max", r))
                    V.tensor_scalar(msm[:, 1, :], msm[:, 0, :], -1.0, None, ALU.mult).then_inc(mpV.did("neg"), 1)
                    dve.wait_ge(mpA.sem, mpA.at("exp", r))
                    V.reciprocal(msm[:, 3, :], msm[:, 2, :]).then_inc(mpV.did("inv"), 1)
                    dve.wait_ge(mpV.sem, mpV.at("inv", r))
                    for t in range(TT):
                        row = msc[:, QO[t]:QO[t] + QW[t]]
                        last = V.tensor_scalar(row, row, msm[:, 3, t:t + 1], None, ALU.mult)
                    last.then_inc(mpV.did("p"), 1)

            ml_round(0, 0, True, False)
            with dve.Fori(0, (MH - 2) // 2) as i:
                ml_round(2 * i + 1, 1, True, True)
                ml_round(2 * i + 2, 0, True, True)
            ml_round(MH - 1, 1, True, True)
            ml_round(MH, 0, False, True)

            with dve.Fori(0, ROUNDS["mg"]) as i:
                r = i + FIRST["mg"]
                dve.wait_ge(mgV.sem, mgV.at("lo", i - 1))
                used(r, 2)
                dve.wait_ge(mgA.sem, mgA.at("g1", i))
                V.tensor_tensor(mga[:, 0, :], bank[2][:, :], mga[:, 0, :], ALU.mult).then_inc(mgV.did("a"), 1)
                used(r, 3)
                V.tensor_tensor(mga[:, 1, :], bank[3][:, :], mga[:, 1, :], ALU.mult).then_inc(mgV.did("b"), 1)
                dve.wait_ge(mgV.sem, mgV.at("b", i))
                V.tensor_tensor(mga[:, 0, :], mga[:, 0, :], mga[:, 1, :], ALU.add).then_inc(mgV.did("sum"), 1)
                dve.wait_ge(mgV.sem, mgV.at("sum", i))
                gh = mgh[:, bass.ds(i, 1), :]
                V.tensor_copy(gh, mga[:, 0:1, :]).then_inc(mgV.did("hi"), 1)
                dve.wait_ge(mgV.sem, mgV.at("hi", i))
                V.tensor_tensor(mgl[:, bass.ds(i, 1), :], mga[:, 0:1, :], f32(gh), ALU.subtract).then_inc(mgV.did("lo"), 1)

            dve.wait_ge(ld_x3, 16)
            residual(w3A, w3V, FIRST["w3"])
            norm(n3, None, cols("fin2", KT), whole=True)

        for s in all_steps:
            assert s.next % s.n == 0 and s.next, s.names


def _feature_slabs(wm):
    k, c = wm.shape
    a = wm.reshape(k // D, KT, P, c // P, P)
    return a.transpose(3, 0, 2, 1, 4).reshape(-1, P, SLAB)


def _token_slabs(wm):
    c = wm.shape[1]
    a = wm.reshape(4, 2, P, c // S, S)
    return a.transpose(3, 0, 2, 1, 4).reshape(-1, P, SLAB)


def _interleave(*lots):
    return np.stack(lots, axis=1).reshape(-1, P, SLAB)


def _pad(a, width=SLAB):
    return np.pad(a, [(0, 0)] * (a.ndim - 1) + [(0, width - a.shape[-1])])


def _weights(i):
    u, v, z = np.split(i["a_w_in"][0], 3, axis=1)
    us, zs = _feature_slabs(u), _feature_slabs(z)
    uz = np.concatenate([us.reshape(-1, 2, P, SLAB), zs.reshape(-1, 2, P, SLAB)], axis=1).reshape(-1, P, SLAB)
    k, va = np.split(i["w_kv"], 2, axis=1)
    q, za = np.split(i["b_w_qz"][0], 2, axis=1)
    at = _interleave(*(_feature_slabs(m) for m in (k, q, va, za)))
    wi = i["w_in_2"][0]
    cuts = np.cumsum([D, D, D, D, QL * P, KL * P, ROPE, D])
    hq, hf, hi, hz, cq, ckv, kr, mz, gl = np.split(wi, cuts, axis=1)
    hg = _interleave(*(_feature_slabs(m) for m in (hq, hf, hi, hz)))

    def swapped(m):
        return np.concatenate([m, m[..., ROPE // 2:], m[..., :ROPE // 2]], axis=-1)

    dn = np.concatenate([_feature_slabs(cq), _feature_slabs(ckv), _feature_slabs(swapped(kr)),
                         np.zeros((2, P, SLAB), wi.dtype)])
    uq = i["w_uq_2"][0].reshape(QL, P, MH, NOPE + ROPE)
    uq = np.concatenate([uq[..., :NOPE], swapped(uq[..., NOPE:])], axis=-1)
    uq = _pad(uq.transpose(2, 1, 0, 3).reshape(MH, P, -1))
    ukv = i["w_ukv_2"][0].reshape(KL, P, MH, 2 * P)
    ukv = _pad(ukv.transpose(2, 1, 0, 3).reshape(MH, P, -1))
    zs = _feature_slabs(mz)
    ml = _interleave(uq, ukv, zs, np.zeros_like(zs))
    g0, g1 = np.split(gl, 2, axis=1)
    mg = _interleave(*(_feature_slabs(m) for m in (g0, g1, i["w_proj_a_2"][0], i["w_proj_b_2"][0])))
    parts = {"v": _token_slabs(v), "uz": uz, "w1": _feature_slabs(i["a_w_out"][0]), "at": at,
             "w2": _feature_slabs(i["b_w_out"][0]), "hg": hg, "dn": dn, "ml": ml, "mg": mg,
             "w3": _feature_slabs(i["w_out_2"][0])}
    for name, rounds in ROUNDS.items():
        assert parts[name].shape[0] == 4 * rounds, name
    return np.concatenate([parts[name] for name in ROUNDS])


def _tables():
    f = np.float32
    p, c = np.arange(P)[:, None], np.arange(S)[None, :]
    consts = np.concatenate([np.eye(P, dtype=f), np.ones((P, P), f), np.full((P, 1), EPS, f)], axis=1)
    starts = np.broadcast_to(np.where(c % HC == 0, f(0), f(1)), (P, S))
    t = c % P
    causal = np.where((p // HC == t // HC) & (p <= t), f(1), f(0))
    later = np.where(c - (S - P) > p, f(NEG), f(0))
    inv = f(10000.0) ** (-np.arange(0, ROPE, 2, dtype=f) / f(ROPE))
    ang = np.arange(S, dtype=f)[None, :] * inv[:, None]
    cos, sin = np.cos(ang), np.sin(ang)
    turn = np.concatenate([cos, cos, -sin, sin])
    return consts, np.stack([starts, causal], axis=1).astype(f), np.stack([later, turn], axis=1).astype(f)


def kernel(**inputs):
    import concourse.bacc as _bacc
    from concourse.bass_utils import run_bass_kernel_spmd as _run

    i = {name: np.asarray(a) for name, a in inputs.items()}
    vecs = [i[n].reshape(-1, P).T for n in ("a_norm_g", "a_ln_g", "a_ln_b", "kv_norm_g", "b_norm_g",
                                            "final_norm_g", "norm_g_2", "b_gate_2")]
    vecs += [i["lb_logits_2"][0].reshape(-1, P).T, i["lb_logits_2"][1].reshape(-1, P).T]
    vecs += [i[n].reshape(-1, P).T for n in ("hg_norm_g_2", "q_a_g_2", "kv_a_g_2", "final_norm_g_2")]
    rel = i["b_rel_bias"][0][:, ::-1]
    consts, masks_hg, masks_ml = _tables()
    arrays = {
        "xt": i["x"][0].T.reshape(KT, P, S).transpose(1, 0, 2),
        "w": _weights(i),
        "vecs": np.concatenate(vecs, axis=1),
        "ws": np.pad(i["a_w_s"][0].transpose(2, 0, 1), ((0, 0), (0, 2), (0, 0))),
        "bs": i["a_b_s"][0],
        "relx": np.pad(rel, ((0, 0), (255, 0)), mode="edge")[:, :RELX],
        "consts": consts, "masks_hg": masks_hg, "masks_ml": masks_ml,
    }
    arrays = {n: np.ascontiguousarray(a) for n, a in arrays.items()}
    nc = _bacc.Bacc("TRN2", target_bir_lowering=False, num_devices=1)
    args = [nc.dram_tensor(n, a.shape, F32, kind="ExternalInput").ap() for n, a in arrays.items()]
    args.append(nc.dram_tensor("x_kept", (P, KT, S), F32, kind="Internal").ap())
    args.append(nc.dram_tensor("rel_tab", (BH + 2, P, S), F32, kind="Internal").ap())
    args.append(nc.dram_tensor("out", (KT, P, S), F32, kind="ExternalOutput").ap())
    build(nc, *args)
    r = _run(nc, [arrays], core_ids=[0])
    return np.asarray(r.results[0]["out"]).reshape(D, S).T.reshape(1, S, D)
```
